# Optimizing a Trainium2 kernel written in Bass

```python
import math
import jax, jax.numpy as jnp
from jax import lax
import numpy as np

D_MODEL = 1024
BATCH = 1
SEQ = 1024
DEPTH = 1

CHUNK = 64
BLOCK = 128
N_META = 16
FRONT = BLOCK
META_START = FRONT - N_META
N_MIXERS = 3
SB_DIM = 128
SB_HEADS = D_MODEL // SB_DIM
DIFF_DIM = 128
DIFF_HEADS = D_MODEL // (2 * DIFF_DIM)
SWA_DIM = 64
SWA_Q_HEADS = D_MODEL // SWA_DIM
SWA_KV_HEADS = SWA_Q_HEADS // 8
SWA_GROUP = SWA_Q_HEADS // SWA_KV_HEADS
WINDOW = 128
WINDOW_CHUNKS = WINDOW // CHUNK
D_FF = 2816
ROPE_THETA = 10000.0
RMS_EPS = 1e-5
NEG = -1e30
HI = lax.Precision.HIGHEST

kernel_name = "hybrid_stickbreak_diff_swa_macaron"

def rmsnorm(x, gain):
    xf = x.astype(jnp.float32)
    y = xf * lax.rsqrt(jnp.mean(xf * xf, axis=-1, keepdims=True) + RMS_EPS)
    return (y * gain.astype(jnp.float32)).astype(x.dtype)

def swiglu_ffn(u, w_in, w_out):
    gate, up = jnp.split(u @ w_in, 2, axis=-1)
    return (jax.nn.silu(gate) * up) @ w_out

def rope_tables(pos, dim):
    inv = 1.0 / (ROPE_THETA ** (jnp.arange(0, dim, 2, dtype=jnp.float32) / dim))
    ang = pos.astype(jnp.float32)[:, None] * inv[None, :]
    ang = jnp.concatenate([ang, ang], axis=-1)
    return jnp.cos(ang), jnp.sin(ang)

def apply_rope(x, cos, sin):
    x1, x2 = jnp.split(x, 2, axis=-1)
    rot = jnp.concatenate([-x2, x1], axis=-1)
    c = cos[None, :, None, :].astype(x.dtype)
    s = sin[None, :, None, :].astype(x.dtype)
    return x * c + rot * s

def stick_breaking_attention(u, w_qkv, w_o, valid):
    b, L, _ = u.shape
    nb = L // BLOCK
    q, k, v = jnp.split(u @ w_qkv, 3, axis=-1)
    q = q.reshape(b, L, SB_HEADS, SB_DIM).transpose(0, 2, 1, 3) * (SB_DIM ** -0.5)
    k = k.reshape(b, L, SB_HEADS, SB_DIM).transpose(0, 2, 1, 3)
    v = v.reshape(b, L, SB_HEADS, SB_DIM).transpose(0, 2, 1, 3)
    idx = jnp.arange(L)
    ar = jnp.arange(BLOCK)
    tri = (ar[None, :] >= ar[:, None]).astype(jnp.float32)
    outs = []
    for n in range(nb):
        lk_len = (n + 1) * BLOCK
        qi, ki = idx[n * BLOCK:lk_len], idx[:lk_len]
        z = jnp.einsum('bhqd,bhkd->bhqk', q[:, :, n * BLOCK:lk_len], k[:, :, :lk_len],
                       preferred_element_type=jnp.float32)
        before = ki[None, :] < qi[:, None]
        log_keep = jnp.where(before, jax.nn.log_sigmoid(-z), 0.0)
        lk = log_keep.reshape(b, SB_HEADS, BLOCK, n + 1, BLOCK)
        within = jnp.einsum('bhqnj,kj->bhqnk', lk, tri, precision=HI)
        an = jnp.arange(n + 1)
        later_mat = (an[:, None] > an[None, :]).astype(jnp.float32)
        later = jnp.einsum('bhqn,nm->bhqm', jnp.sum(lk, axis=-1), later_mat, precision=HI)
        log_w = z + (within + later[..., None]).reshape(b, SB_HEADS, BLOCK, lk_len)
        w = jnp.where((before & valid[:lk_len][None, :])[None, None], jnp.exp(log_w), 0.0)
        outs.append(jnp.einsum('bhqk,bhkd->bhqd', w.astype(v.dtype), v[:, :, :lk_len]))
    o = jnp.concatenate(outs, axis=2).transpose(0, 2, 1, 3).reshape(b, L, SB_HEADS * SB_DIM)
    return o @ w_o

def differential_attention(u, w_qkv, lam_params, subln, w_o, cos, sin, cid, valid, lambda_init):
    b, L, _ = u.shape
    nb = L // BLOCK
    q, k, v = jnp.split(u @ w_qkv, 3, axis=-1)
    q = apply_rope(q.reshape(b, L, 2 * DIFF_HEADS, DIFF_DIM), cos, sin) * (DIFF_DIM ** -0.5)
    k = apply_rope(k.reshape(b, L, 2 * DIFF_HEADS, DIFF_DIM), cos, sin)
    q = q.reshape(b, L, DIFF_HEADS, 2, DIFF_DIM).transpose(0, 2, 3, 1, 4)
    k = k.reshape(b, L, DIFF_HEADS, 2, DIFF_DIM).transpose(0, 2, 3, 1, 4)
    v = v.reshape(b, L, DIFF_HEADS, 2 * DIFF_DIM).transpose(0, 2, 1, 3)
    lp = lam_params.astype(jnp.float32)
    lam = jnp.exp(jnp.sum(lp[0] * lp[1])) - jnp.exp(jnp.sum(lp[2] * lp[3])) + lambda_init
    outs = []
    for n in range(nb):
        lk_len = (n + 1) * BLOCK
        s = jnp.einsum('bhmqd,bhmkd->bhmqk', q[:, :, :, n * BLOCK:lk_len], k[:, :, :, :lk_len],
                       preferred_element_type=jnp.float32)
        allowed = valid[:lk_len][None, :] & (cid[:lk_len][None, :] <= cid[n * BLOCK:lk_len][:, None])
        p = jax.nn.softmax(jnp.where(allowed[None, None, None], s, NEG), axis=-1)
        a = p[:, :, 0] - lam * p[:, :, 1]
        outs.append(jnp.einsum('bhqk,bhkd->bhqd', a.astype(v.dtype), v[:, :, :lk_len]))
    o = jnp.concatenate(outs, axis=2).transpose(0, 2, 1, 3)
    o = rmsnorm(o, subln) * (1.0 - lambda_init)
    return o.reshape(b, L, DIFF_HEADS * 2 * DIFF_DIM) @ w_o

def sliding_window_sink_attention(u, w_qkv, sinks, w_o, cos, sin, cid):
    b, L, _ = u.shape
    nb = L // BLOCK
    qd, kd = SWA_Q_HEADS * SWA_DIM, SWA_KV_HEADS * SWA_DIM
    q, k, v = jnp.split(u @ w_qkv, [qd, qd + kd], axis=-1)
    q = apply_rope(q.reshape(b, L, SWA_Q_HEADS, SWA_DIM), cos, sin) * (SWA_DIM ** -0.5)
    k = apply_rope(k.reshape(b, L, SWA_KV_HEADS, SWA_DIM), cos, sin)
    v = v.reshape(b, L, SWA_KV_HEADS, SWA_DIM)
    qb = q.reshape(b, nb, BLOCK, SWA_KV_HEADS, SWA_GROUP, SWA_DIM)
    kb = k.reshape(b, nb, BLOCK, SWA_KV_HEADS, SWA_DIM)
    vb = v.reshape(b, nb, BLOCK, SWA_KV_HEADS, SWA_DIM)
    k_band = jnp.concatenate([jnp.roll(kb, 1, axis=1), kb], axis=2)
    v_band = jnp.concatenate([jnp.roll(vb, 1, axis=1), vb], axis=2)
    k_meta, v_meta = k[:, META_START:FRONT], v[:, META_START:FRONT]
    cq = cid.reshape(nb, BLOCK)
    c_band = jnp.concatenate([jnp.roll(cq, 1, axis=0), cq], axis=1)
    ck, cqq = c_band[:, None, :], cq[:, :, None]
    band_ok = (ck >= 1) & (ck <= cqq) & (ck >= cqq - (WINDOW_CHUNKS - 1))
    s_band = jnp.einsum('bnqhgd,bnkhd->bnhgqk', qb, k_band, preferred_element_type=jnp.float32)
    s_band = jnp.where(band_ok[None, :, None, None], s_band, NEG)
    s_meta = jnp.einsum('bnqhgd,bmhd->bnhgqm', qb, k_meta, preferred_element_type=jnp.float32)
    sink = jnp.broadcast_to(
        sinks.astype(jnp.float32).reshape(SWA_KV_HEADS, SWA_GROUP)[None, None, :, :, None, None],
        s_meta.shape[:-1] + (1,))
    p = jax.nn.softmax(jnp.concatenate([s_meta, s_band, sink], axis=-1), axis=-1)
    p_meta = p[..., :N_META].astype(v.dtype)
    p_band = p[..., N_META:N_META + 2 * BLOCK].astype(v.dtype)
    o = (jnp.einsum('bnhgqm,bmhd->bnqhgd', p_meta, v_meta)
         + jnp.einsum('bnhgqk,bnkhd->bnqhgd', p_band, v_band))
    return o.reshape(b, L, qd) @ w_o

def setup_inputs(seed: int = 0) -> dict:
    key = jax.random.key(seed)
    ks = jax.random.split(key, 19)
    n_sb = len(range(0, DEPTH, N_MIXERS))
    n_diff = len(range(1, DEPTH, N_MIXERS))
    n_swa = len(range(2, DEPTH, N_MIXERS))

    def normal(k, shape, scale):
        return scale * jax.random.normal(k, shape, jnp.float32)

    def gain(k, shape):
        return 1.0 + 0.02 * jax.random.normal(k, shape, jnp.float32)

    swa_cols = (SWA_Q_HEADS + 2 * SWA_KV_HEADS) * SWA_DIM
    return {
        "x": normal(ks[0], (BATCH, SEQ, D_MODEL), 1.0),
        "meta_tokens": normal(ks[1], (N_META, D_MODEL), 1.0),
        "ffn1_norm": gain(ks[2], (DEPTH, D_MODEL)),
        "ffn1_w_in": normal(ks[3], (DEPTH, D_MODEL, 2 * D_FF), D_MODEL ** -0.5),
        "ffn1_w_out": normal(ks[4], (DEPTH, D_FF, D_MODEL), D_FF ** -0.5),
        "mix_norm": gain(ks[5], (DEPTH, D_MODEL)),
        "ffn2_norm": gain(ks[6], (DEPTH, D_MODEL)),
        "ffn2_w_in": normal(ks[7], (DEPTH, D_MODEL, 2 * D_FF), D_MODEL ** -0.5),
        "ffn2_w_out": normal(ks[8], (DEPTH, D_FF, D_MODEL), D_FF ** -0.5),
        "sb_w_qkv": normal(ks[9], (n_sb, D_MODEL, 3 * SB_HEADS * SB_DIM), D_MODEL ** -0.5),
        "sb_w_o": normal(ks[10], (n_sb, SB_HEADS * SB_DIM, D_MODEL), D_MODEL ** -0.5),
        "diff_w_qkv": normal(ks[11], (n_diff, D_MODEL, 3 * DIFF_HEADS * 2 * DIFF_DIM), D_MODEL ** -0.5),
        "diff_lambda": normal(ks[12], (n_diff, 4, DIFF_DIM), 0.1),
        "diff_subln": gain(ks[13], (n_diff, 2 * DIFF_DIM)),
        "diff_w_o": normal(ks[14], (n_diff, DIFF_HEADS * 2 * DIFF_DIM, D_MODEL), D_MODEL ** -0.5),
        "swa_w_qkv": normal(ks[15], (n_swa, D_MODEL, swa_cols), D_MODEL ** -0.5),
        "swa_sinks": normal(ks[16], (n_swa, SWA_Q_HEADS), 0.5),
        "swa_w_o": normal(ks[17], (n_swa, SWA_Q_HEADS * SWA_DIM, D_MODEL), D_MODEL ** -0.5),
        "final_norm": gain(ks[18], (D_MODEL,)),
    }

def reference(x, meta_tokens, ffn1_norm, ffn1_w_in, ffn1_w_out, mix_norm, ffn2_norm, ffn2_w_in,
              ffn2_w_out, sb_w_qkv, sb_w_o, diff_w_qkv, diff_lambda, diff_subln, diff_w_o,
              swa_w_qkv, swa_sinks, swa_w_o, final_norm):
    b = x.shape[0]
    pad = jnp.zeros((b, META_START, D_MODEL), x.dtype)
    meta = jnp.broadcast_to(meta_tokens.astype(x.dtype)[None], (b, N_META, D_MODEL))
    h = jnp.concatenate([pad, meta, x], axis=1)
    L = h.shape[1]
    idx = jnp.arange(L)
    cid = (idx - FRONT) // CHUNK + 1
    valid = idx >= META_START
    pos = idx - META_START
    cos_d, sin_d = rope_tables(pos, DIFF_DIM)
    cos_w, sin_w = rope_tables(pos, SWA_DIM)

    for i in range(DEPTH):
        h = h + 0.5 * swiglu_ffn(rmsnorm(h, ffn1_norm[i]), ffn1_w_in[i], ffn1_w_out[i])
        u = rmsnorm(h, mix_norm[i])
        kind, j = i % N_MIXERS, i // N_MIXERS
        if kind == 0:
            y = stick_breaking_attention(u, sb_w_qkv[j], sb_w_o[j], valid)
        elif kind == 1:
            lambda_init = 0.8 - 0.6 * math.exp(-0.3 * i)
            y = differential_attention(u, diff_w_qkv[j], diff_lambda[j], diff_subln[j], diff_w_o[j],
                                       cos_d, sin_d, cid, valid, lambda_init)
        else:
            y = sliding_window_sink_attention(u, swa_w_qkv[j], swa_sinks[j], swa_w_o[j],
                                              cos_w, sin_w, cid)
        h = h + y
        h = h + 0.5 * swiglu_ffn(rmsnorm(h, ffn2_norm[i]), ffn2_w_in[i], ffn2_w_out[i])

    h = rmsnorm(h, final_norm)
    return h[:, FRONT:]


_drawn_inputs = setup_inputs


def setup_inputs(seed=0):
    import zlib

    import numpy as np

    out = dict(_drawn_inputs(seed))
    spreads = {}
    factors = {'meta_tokens': 3.045,
     'ffn1_norm': 6.193,
     'mix_norm': 4.176,
     'ffn2_norm': 8.0,
     'final_norm': 2.901}
    for name, (base, spread) in spreads.items():
        noise = np.random.default_rng([zlib.crc32(name.encode()), seed]).standard_normal(out[name].shape)
        drawn = base * np.exp(spread * noise) if base else spread * noise
        out[name] = __import__('jax').numpy.asarray(drawn.astype(out[name].dtype))
    for name, factor in factors.items():
        out[name] = (out[name] * factor).astype(out[name].dtype)
    return out
```

```python
from contextlib import ExitStack

import concourse.bass as bass
from concourse import mybir

F32 = mybir.dt.float32
F32R = mybir.dt.float32r
ALU = mybir.AluOpType
ACT = mybir.ActivationFunctionType

P = 128
BANK = 512
FRAMES, META, D_MODEL = 1024, 16, 1024
TOKENS = FRAMES + META
KT = D_MODEL // P
D_FF = 2816
FF_PAIRS = D_FF // (2 * P)
HEADS = 8
EPS = 1e-5
Q_SCALE = float(P) ** -0.5
NEG = -1e30

ALL_CHUNKS = [(0, 348), (348, 348), (696, 344)]
FRAME_CHUNKS = [(0, BANK), (BANK, BANK)]

META_TILE = FRAMES // P


def attention_steps():
    steps = []
    for chunk in (1, 0):
        q_begin, q_end = chunk * BANK, (chunk + 1) * BANK
        for tile in range(q_end // P - 1, -1, -1):
            first = min(max(tile * P, q_begin), q_end - 2 * P)
            mask = None if tile * P < q_begin else P - (tile * P - first)
            steps.append((chunk, tile, first, q_end - first, mask))
        steps.append((chunk, META_TILE, q_begin, BANK, None))
    return steps


STEPS = attention_steps()
S = len(STEPS)
COMPLETIONS = sum(tile != META_TILE for _, tile, _, _, _ in STEPS)
LAST_OF_CHUNK = {chunk: max(t for t in range(S) if STEPS[t][0] == chunk) for chunk in (0, 1)}
SLOTS = S + 3

G_V, G_Q1, G_K, G_VT, G_Q0, G_O = 0, 3, 4, 7, 10, 11
GROUPS_FIRST, GROUPS = 11, 27
VT_GROUPS = [(0, 4), (4, 8), (8, 9)]
Q0_SLOTS = 4


def o_groups(slot, place):
    if slot < Q0_SLOTS:
        return []
    if slot < Q0_SLOTS + 4:
        return [2 * (slot - Q0_SLOTS) + place]
    return [8 + slot - 8] if place == 1 and slot < 16 else []


def group_base(h):
    return 0 if isinstance(h, int) and h == 0 else GROUPS * h - (GROUPS - GROUPS_FIRST)


def completions_before(t):
    return sum(STEPS[s][1] != META_TILE for s in range(t))


def wait(engine, semaphore, value):
    if isinstance(value, int) and value <= 0:
        return
    engine.wait_ge(semaphore, value)


def build(nc, x, meta, gains_in, w1_in, w1_out, w2_in, w2_out, w_qkv, w_o, g_final, out):
    ctx = ExitStack()
    with ctx:
        def sbuf(name, shape, dtype):
            return ctx.enter_context(nc.sbuf_tensor(name, shape, dtype))

        def sem(name):
            return ctx.enter_context(nc.semaphore(name))

        h = sbuf("h", [P, KT, TOKENS], F32)
        u_hi = sbuf("u_hi", [P, KT, TOKENS], F32R)
        u_lo = sbuf("u_lo", [P, KT, TOKENS], F32R)
        scratch = sbuf("scratch", [P, 8192], F32)
        work = sbuf("work", [P, 18720], F32R)
        tri = sbuf("tri", [P, P], F32R)
        tri_rest = sbuf("tri_rest", [P, P], F32R)
        ident_r = sbuf("ident_r", [P, P], F32R)
        mask = sbuf("mask", [P, 3 * P], F32R)
        ident = sbuf("ident", [P, P], F32)
        ones = sbuf("ones", [P, P], F32)
        gains = sbuf("gains", [P, 3, KT], F32)
        stats = sbuf("stats", [P, KT, 4], F32)
        eps = sbuf("eps", [P, 1], F32)
        psum = ctx.enter_context(nc.psum_tensor("psum", [P, 8, BANK], F32))

        def piece(arena, at, *dims):
            size = 1
            for n in dims:
                size *= n
            flat = arena[:, at:at + size]
            if len(dims) == 2:
                return flat.rearrange("p (a b) -> p a b", a=dims[0])
            if len(dims) == 3:
                return flat.rearrange("p (a b c) -> p a b c", a=dims[0], b=dims[1])
            return flat

        x_tiles = piece(scratch, 4096, 4, D_MODEL)
        sq = piece(scratch, 4096, 3, BANK)
        rstd = piece(scratch, 5632, 2, BANK)
        un = piece(scratch, 6656, 3, BANK)
        stage_g = piece(scratch, 0, KT, 2 * P)
        stage_u = piece(scratch, 2048, KT, 2 * P)
        stage_d = piece(scratch, 4096, 2, D_MODEL)
        silu_g = piece(scratch, 6144, 2, BANK)
        hidden = piece(scratch, 7168, 2, BANK)
        stage_a = piece(scratch, 0, 2, D_MODEL)
        zs = piece(scratch, 2048, 4, BANK)
        sp = piece(scratch, 4096, 3, BANK)
        wf = piece(scratch, 5632, 2, BANK)
        v_t = piece(scratch, 6656, TOKENS)
        out_tiles = piece(scratch, 0, 4, D_MODEL)
        gain_row = piece(scratch, 4096, D_MODEL)
        square_out = piece(scratch, 6144, 2, BANK)

        wg = piece(work, 0, 2, KT, 2 * P)
        wu = piece(work, 4096, 2, KT, 2 * P)
        wd = piece(work, 8192, 2, 2, D_MODEL)
        hid_hi = piece(work, 12288, 2, TOKENS)
        hid_lo = piece(work, 14368, 2, TOKENS)
        wq = piece(work, 0, 2, KT, P)
        w_kv = piece(work, 2048, 2, KT, P)
        wo = piece(work, 4096, 2, D_MODEL)
        q = piece(work, 6144, 2, FRAMES)
        k = piece(work, 8192, 2, TOKENS)
        v = piece(work, 10272, 2, META_TILE + 1, P)
        o = piece(work, 12576, 2, FRAMES)
        sp_hi = piece(work, 14624, 2, BANK)
        sp_lo = piece(work, 15648, 2, BANK)
        w_hi = piece(work, 16672, 2, BANK)
        w_lo = piece(work, 17696, 2, BANK)

        const_set = sem("const_set")
        gains_loaded = sem("gains_loaded")
        x_loaded = [sem(f"x_loaded{i}") for i in range(4)]
        x_transposed = sem("x_transposed")
        h_low = sem("h_low")
        h_high = sem("h_high")
        norms = [{name: sem(f"norm{n}_{name}") for name in
                  ("squared", "summed", "root", "rstd", "un", "hi", "lo")} for n in range(3)]
        ffns = [{name: sem(f"ffn{n}_{name}") for name in
                 ("g_loaded", "u_loaded", "d_loaded", "g_hi", "u_hi", "d_hi", "g_split", "u_split",
                  "d_split", "gate", "up", "silu", "hidden", "hid_hi", "hid_lo", "down", "added")}
                for n in range(2)]
        a_loaded = [sem(f"a_loaded{i}") for i in range(2)]
        a_hi = sem("a_hi")
        a_split = sem("a_split")
        grouped = sem("grouped")
        evacuated = sem("evacuated")
        proj_hi = sem("proj_hi")
        scored = sem("scored")
        z_read = sem("z_read")
        eps_set = sem("eps_set")
        exped = sem("exped")
        logged = sem("logged")
        softplused = sem("softplused")
        sp_hi_done = sem("sp_hi_done")
        sp_lo_done = sem("sp_lo_done")
        summed = sem("summed")
        completed = sem("completed")
        logw_done = sem("logw_done")
        w_done = sem("w_done")
        w_hi_done = sem("w_hi_done")
        w_lo_done = sem("w_lo_done")
        weighed = sem("weighed")
        o_hi_done = sem("o_hi_done")
        o_lo_done = sem("o_lo_done")
        gain_loaded = sem("gain_loaded")
        out_transposed = sem("out_transposed")
        out_squared = sem("out_squared")
        out_total = sem("out_total")
        out_root = sem("out_root")
        out_rstd = sem("out_rstd")
        out_scaled = sem("out_scaled")
        out_stored = [sem(f"out_stored{i}") for i in range(4)]

        CONSTANTS = 8
        NORM_BANK = 3

        def attention_over(engine):
            engine.wait_ge(evacuated, GROUPS_FIRST + GROUPS * (HEADS - 1) + 16)

        def ffn_over(engine, n):
            chunks = len(ALL_CHUNKS) if n == 0 else len(FRAME_CHUNKS)
            engine.wait_ge(ffns[n]["added"], FF_PAIRS * chunks * KT)

        def norm_over(engine, n):
            engine.wait_ge(norms[n]["lo"], KT * (len(FRAME_CHUNKS) if n == 2 else len(ALL_CHUNKS)))

        block = ctx.enter_context(nc.Block())

        @block.sync
        def _(sp_eng):
            def load_x(t):
                rows = META if t == META_TILE else P
                src = meta[:, :] if t == META_TILE else x[t * P:(t + 1) * P, :]
                if t >= 4:
                    sp_eng.wait_ge(x_transposed, t - 3)
                sp_eng.dma_start(x_tiles[0:rows, t % 4, :], src).then_inc(x_loaded[t % 4], 16)

            def ffn_sources(n, i):
                w_in, w_out = (w1_in, w1_out) if n == 0 else (w2_in, w2_out)
                gate = w_in[:, bass.ds(i * (2 * P), 2 * P)].rearrange("(k p) f -> p k f", p=P)
                up = w_in[:, bass.ds((i + FF_PAIRS) * (2 * P), 2 * P)].rearrange("(k p) f -> p k f", p=P)
                down = w_out[bass.ds(i * (2 * P), 2 * P), :].rearrange("(t p) d -> p t d", p=P)
                return gate, up, down

            def ffn_rest(n):
                s = ffns[n]
                with sp_eng.Fori(1, FF_PAIRS) as i:
                    gate, up, down = ffn_sources(n, i)
                    sp_eng.wait_ge(s["g_split"], i)
                    sp_eng.dma_start(stage_g, gate).then_inc(s["g_loaded"], 16)
                    sp_eng.wait_ge(s["u_split"], i)
                    sp_eng.dma_start(stage_u, up).then_inc(s["u_loaded"], 16)
                    sp_eng.wait_ge(s["d_split"], i)
                    sp_eng.dma_start(stage_d, down).then_inc(s["d_loaded"], 16)

            for t in range(4):
                load_x(t)
            gate, up, down = ffn_sources(0, 0)
            sp_eng.dma_start(stage_g, gate).then_inc(ffns[0]["g_loaded"], 16)
            for t in range(4, 9):
                load_x(t)
            sp_eng.dma_start(stage_u, up).then_inc(ffns[0]["u_loaded"], 16)
            sp_eng.dma_start(gains[:], gains_in[:, :, :]).then_inc(gains_loaded, 16)
            sp_eng.wait_ge(norms[0]["lo"], len(ALL_CHUNKS) * KT)
            sp_eng.dma_start(stage_d, down).then_inc(ffns[0]["d_loaded"], 16)
            ffn_rest(0)

            def load_a(unit, kind, head):
                slot = unit[0] % 2
                if kind == 3:
                    src = w_o[bass.ds(head * P, P), :]
                else:
                    src = w_qkv[:, bass.ds((head + kind * HEADS) * P, P)].rearrange("(k p) f -> p k f", p=P)
                dst = stage_a[:, slot, :]
                if kind != 3:
                    dst = dst.rearrange("p (k f) -> p k f", k=KT)
                wait(sp_eng, a_split, unit[0] - 1 + 4 * unit[1])
                sp_eng.dma_start(dst, src).then_inc(a_loaded[slot], 16)

            sp_eng.wait_ge(ffns[0]["g_split"], FF_PAIRS)
            load_a((0, 0), 2, 0)
            load_a((1, 0), 0, 0)
            load_a((2, 0), 1, 0)
            with sp_eng.Fori(0, HEADS - 1) as hd:
                load_a((3, hd), 2, hd + 1)
                load_a((4, hd), 0, hd + 1)
                load_a((5, hd), 3, hd)
                load_a((6, hd), 1, hd + 1)
            load_a((3, HEADS - 1), 3, HEADS - 1)

            attention_over(sp_eng)
            gate, up, down = ffn_sources(1, 0)
            sp_eng.dma_start(stage_g, gate).then_inc(ffns[1]["g_loaded"], 16)
            sp_eng.dma_start(stage_u, up).then_inc(ffns[1]["u_loaded"], 16)
            sp_eng.wait_ge(norms[2]["lo"], len(FRAME_CHUNKS) * KT)
            sp_eng.dma_start(stage_d, down).then_inc(ffns[1]["d_loaded"], 16)
            ffn_rest(1)

            sp_eng.wait_ge(ffns[1]["d_split"], FF_PAIRS)
            sp_eng.dma_start(gain_row, g_final.rearrange("(a n) -> a n", a=1).to_broadcast([P, D_MODEL]))\
                .then_inc(gain_loaded, 16)
            for t in range(FRAMES // P):
                sp_eng.wait_ge(out_scaled, 2 * (t + 1))
                sp_eng.dma_start(out[t * P:(t + 1) * P, :], out_tiles[:, t % 4, :]).then_inc(out_stored[t % 4], 16)
            for slot in range(4):
                sp_eng.wait_ge(out_stored[slot], 16 * (FRAMES // P // 4))

        @block.gpsimd
        def _(pool):
            nc.gpsimd.memset(ident[:], 0.0).then_inc(const_set, 1)
            nc.gpsimd.memset(ones[:], 1.0).then_inc(const_set, 1)
            nc.gpsimd.memset(h[:, 0, 0:3 * P], 0.0).then_inc(const_set, 1)
            pool.wait_ge(const_set, 3)
            nc.gpsimd.affine_select(out=ident[:], in_=ident[:], compare_op=ALU.not_equal, fill=1.0, base=0,
                                    pattern=[[-1, P]], channel_multiplier=1).then_inc(const_set, 1)
            nc.gpsimd.affine_select(out=tri[:], in_=ones[:], compare_op=ALU.is_ge, fill=0.0, base=0,
                                    pattern=[[-1, P]], channel_multiplier=1).then_inc(const_set, 1)
            nc.gpsimd.affine_select(out=tri_rest[:], in_=ones[:], compare_op=ALU.is_gt, fill=0.0, base=0,
                                    pattern=[[1, P]], channel_multiplier=-1).then_inc(const_set, 1)
            nc.gpsimd.affine_select(out=mask[:], in_=h[:, 0, 0:3 * P], compare_op=ALU.is_gt, fill=NEG, base=-P,
                                    pattern=[[1, 3 * P]], channel_multiplier=-1).then_inc(const_set, 1)
            pool.wait_ge(const_set, 4)
            nc.gpsimd.tensor_copy(ident_r[:], ident[:]).then_inc(const_set, 1)

            def ffn(n):
                s = ffns[n]

                def split_gate_up(turn):
                    pool.wait_ge(s["g_hi"], turn + 1)
                    nc.gpsimd.tensor_tensor(wg[:, 1], stage_g, wg[:, 0].bitcast(F32), ALU.subtract)\
                        .then_inc(s["g_split"], 1)
                    pool.wait_ge(s["u_hi"], turn + 1)
                    nc.gpsimd.tensor_tensor(wu[:, 1], stage_u, wu[:, 0].bitcast(F32), ALU.subtract)\
                        .then_inc(s["u_split"], 1)

                def split_down(turn):
                    pool.wait_ge(s["d_hi"], turn + 1)
                    nc.gpsimd.tensor_tensor(wd[:, 1], stage_d, wd[:, 0].bitcast(F32), ALU.subtract)\
                        .then_inc(s["d_split"], 1)

                split_gate_up(0)
                with pool.Fori(0, FF_PAIRS - 1) as i:
                    split_down(i)
                    split_gate_up(i + 1)
                split_down(FF_PAIRS - 1)

            ffn(0)

            def split_weights(unit, kind):
                dst = (wq, w_kv, w_kv, wo)[kind]
                src = stage_a[:, unit[0] % 2, :]
                if kind != 3:
                    src = src.rearrange("p (k f) -> p k f", k=KT)
                pool.wait_ge(a_hi, unit[0] + 1 + 4 * unit[1])
                nc.gpsimd.tensor_tensor(dst[:, 1], src, dst[:, 0].bitcast(F32), ALU.subtract)\
                    .then_inc(a_split, 1)

            def head(hd, last):
                for s in range(SLOTS):
                    if s < S:
                        n, rows = STEPS[s][3], META if STEPS[s][1] == META_TILE else P
                        pool.wait_ge(sp_hi_done, S * hd + s + 1)
                        nc.gpsimd.tensor_tensor(sp_lo[0:rows, s % 2, 0:n], sp[0:rows, s % 3, 0:n],
                                                sp_hi[0:rows, s % 2, 0:n].bitcast(F32), ALU.subtract)\
                            .then_inc(sp_lo_done, 1)
                    if 2 <= s < S + 2:
                        t = s - 2
                        n, rows = STEPS[t][3], META if STEPS[t][1] == META_TILE else P
                        pool.wait_ge(w_hi_done, S * hd + t + 1)
                        nc.gpsimd.tensor_tensor(w_lo[0:rows, t % 2, 0:n], wf[0:rows, t % 2, 0:n],
                                                w_hi[0:rows, t % 2, 0:n].bitcast(F32), ALU.subtract)\
                            .then_inc(w_lo_done, 1)
                    if s == 5 and not last:
                        split_weights((3, hd), 2)
                    if s == 7 and not last:
                        split_weights((4, hd), 0)
                if last:
                    split_weights((3, hd), 3)
                else:
                    split_weights((5, hd), 3)
                    split_weights((6, hd), 1)

            split_weights((0, 0), 2)
            split_weights((1, 0), 0)
            split_weights((2, 0), 1)
            with pool.Fori(0, HEADS - 1) as hd:
                head(hd, last=False)
            head(HEADS - 1, last=True)

            ffn(1)

        @block.scalar
        def _(act):
            for t in range(9):
                cols = META if t == META_TILE else P
                act.wait_ge(x_transposed, t + 1)
                b = (2 * t + 1) % 8
                src = psum[:, b, :].rearrange("p (k c) -> p k c", k=4)[:, :, 0:cols]
                nc.scalar.activation(h[:, 4:8, t * P:t * P + cols], src, ACT.Copy).then_inc(h_high, 1)

            def norm(n, chunks, meanwhile):
                s = norms[n]

                def square(c, kt):
                    m, (at, cols) = c * KT + kt, chunks[c]
                    wait(act, s["summed"], m - 2)
                    nc.scalar.activation(sq[:, m % 3, 0:cols], h[:, kt, at:at + cols], ACT.Square)\
                        .then_inc(s["squared"], 1)

                def root(c):
                    cols = chunks[c][1]
                    act.wait_ge(s["summed"], KT * (c + 1))
                    if c >= 2:
                        act.wait_ge(s["un"], KT * (c - 1))
                    nc.scalar.activation(rstd[:, c % 2, 0:cols], psum[:, NORM_BANK + c, 0:cols], ACT.Sqrt,
                                         scale=1.0 / D_MODEL, bias=eps[:, 0:1]).then_inc(s["root"], 1)

                def hi(c, kt):
                    m, (at, cols) = c * KT + kt, chunks[c]
                    act.wait_ge(s["un"], m + 1)
                    nc.scalar.activation(u_hi[:, kt, at:at + cols], un[:, m % 3, 0:cols], ACT.Copy)\
                        .then_inc(s["hi"], 1)

                for c in (0, 1):
                    for kt in range(KT):
                        square(c, kt)
                meanwhile()
                root(0)
                for kt in range(KT):
                    if len(chunks) > 2:
                        square(2, kt)
                    hi(0, kt)
                for c in range(1, len(chunks)):
                    root(c)
                    for kt in range(KT):
                        hi(c, kt)
                norm_over(act, n)

            def split_gate_up(n, turn):
                s = ffns[n]
                act.wait_ge(s["g_loaded"], 16 * turn + 16)
                nc.scalar.activation(wg[:, 0], stage_g, ACT.Copy).then_inc(s["g_hi"], 1)
                act.wait_ge(s["u_loaded"], 16 * turn + 16)
                nc.scalar.activation(wu[:, 0], stage_u, ACT.Copy).then_inc(s["u_hi"], 1)

            def ffn(n, chunks):
                s = ffns[n]
                per_turn = 2 * len(chunks)

                def turn(i, last):
                    for c, (at, cols) in enumerate(chunks):
                        for ft in range(2):
                            m = 2 * c + ft
                            act.wait_ge(s["gate"], per_turn * i + m + 1)
                            nc.scalar.activation(silu_g[:, m % 2, 0:cols], psum[:, 2 * (m % 2), 0:cols], ACT.Silu)\
                                .then_inc(s["silu"], 1)
                            act.wait_ge(s["hidden"], per_turn * i + m + 1)
                            nc.scalar.activation(hid_hi[:, ft, at:at + cols], hidden[:, m % 2, 0:cols], ACT.Copy)\
                                .then_inc(s["hid_hi"], 1)
                            if m == 0:
                                act.wait_ge(s["d_loaded"], 16 * i + 16)
                                nc.scalar.activation(wd[:, 0], stage_d, ACT.Copy).then_inc(s["d_hi"], 1)
                    if not last:
                        split_gate_up(n, i + 1)

                with act.Fori(0, FF_PAIRS - 1) as i:
                    turn(i, last=False)
                turn(FF_PAIRS - 1, last=True)

            act.wait_ge(h_low, 9)
            act.wait_ge(h_high, 9)
            act.wait_ge(eps_set, 1)
            norm(0, ALL_CHUNKS, lambda: split_gate_up(0, 0))
            ffn(0, ALL_CHUNKS)

            def split_weights(unit, kind):
                dst = (wq, w_kv, w_kv, wo)[kind]
                index = unit[0] + 4 * unit[1]
                src = stage_a[:, unit[0] % 2, :]
                if kind != 3:
                    src = src.rearrange("p (k f) -> p k f", k=KT)
                act.wait_ge(a_loaded[unit[0] % 2], 16 * (unit[0] // 2 + 1) + 32 * unit[1])
                nc.scalar.activation(dst[:, 0], src, ACT.Copy).then_inc(a_hi, 1)

            def head(hd, first, last):
                base = group_base(hd)

                def group_ready(g):
                    act.wait_ge(grouped, base + g + 1)

                group_ready(G_V + 2)
                split_weights((2, 0) if first else (6, hd - 1), 1)
                group_ready(G_Q1)
                nc.scalar.activation(q[:, 0, BANK:], psum[:, 6 + G_Q1 % 2, :], ACT.Copy, scale=Q_SCALE)\
                    .then_inc(proj_hi, 1)
                for c, (at, cols) in enumerate(ALL_CHUNKS):
                    group_ready(G_K + c)
                    nc.scalar.activation(k[:, 0, at:at + cols], psum[:, 6 + (G_K + c) % 2, 0:cols], ACT.Copy)\
                        .then_inc(proj_hi, 1)
                for c, (t0, t1) in enumerate(VT_GROUPS):
                    rows = META if t0 == META_TILE else P
                    group_ready(G_VT + c)
                    src = psum[0:rows, 6 + (G_VT + c) % 2, 0:(t1 - t0) * P].rearrange("p (t d) -> p t d", d=P)
                    nc.scalar.activation(v[0:rows, 0, t0:t1, :], src, ACT.Copy).then_inc(proj_hi, 1)
                for s in range(SLOTS):
                    if s < S:
                        _, tile, _, n, _ = STEPS[s]
                        rows = META if tile == META_TILE else P
                        z, z_sb, e = psum[0:rows, s % 2, 0:n], zs[0:rows, s % 4, 0:n], sp[0:rows, s % 3, 0:n]
                        act.wait_ge(scored, S * hd + s + 1)
                        wait(act, w_done, S * hd + (s - 3 if s >= 4 else 0))
                        nc.scalar.activation(z_sb, z, ACT.Copy).then_inc(z_read, 1)
                        wait(act, sp_lo_done, S * hd + (s - 2 if s >= 3 else 0))
                        nc.scalar.activation(e, z, ACT.Abs).then_inc(z_read, 1)
                        act.wait_ge(z_read, 2 * (S * hd + s + 1))
                        nc.scalar.activation(e, e, ACT.Exp, scale=-1.0).then_inc(exped, 1)
                        act.wait_ge(exped, S * hd + s + 1)
                        nc.scalar.activation(e, e, ACT.Ln, bias=1.0).then_inc(logged, 1)
                    if 2 <= s < S + 2:
                        t = s - 2
                        n, rows = STEPS[t][3], META if STEPS[t][1] == META_TILE else P
                        act.wait_ge(logw_done, S * hd + t + 1)
                        wait(act, w_lo_done, S * hd + (t - 1 if t >= 2 else 0))
                        nc.scalar.activation(wf[0:rows, t % 2, 0:n], zs[0:rows, t % 4, 0:n], ACT.Exp)\
                            .then_inc(w_done, 1)
                    if s == Q0_SLOTS - 1:
                        group_ready(G_Q0)
                        nc.scalar.activation(q[:, 0, 0:BANK], psum[:, 6 + G_Q0 % 2, :], ACT.Copy, scale=Q_SCALE)\
                            .then_inc(proj_hi, 1)
                    if s == 5 and not last:
                        split_weights((3, hd), 2)
                    if s == 7 and not last:
                        split_weights((4, hd), 0)
                    for chunk, slot in ((1, LAST_OF_CHUNK[1] + 4), (0, SLOTS - 1)):
                        if s == slot:
                            act.wait_ge(weighed, S * hd + LAST_OF_CHUNK[chunk] + 1)
                            nc.scalar.activation(o[:, 0, chunk * BANK:(chunk + 1) * BANK], psum[:, 4 + chunk, :],
                                                 ACT.Copy).then_inc(o_hi_done, 1)
                if not first:
                    group_ready(GROUPS - 1)
                split_weights((3, hd) if last else (5, hd), 3)

            def split_first_weights():
                split_weights((0, 0), 2)
                split_weights((1, 0), 0)

            ffn_over(act, 0)
            norm(1, ALL_CHUNKS, split_first_weights)
            head(0, first=True, last=False)
            with act.Fori(1, HEADS - 1) as hd:
                head(hd, first=False, last=False)
            head(HEADS - 1, first=False, last=True)

            attention_over(act)
            norm(2, FRAME_CHUNKS, lambda: split_gate_up(1, 0))
            ffn(1, FRAME_CHUNKS)
            ffn_over(act, 1)

            for t in range(FRAMES // P):
                for half in range(2):
                    m = 2 * t + half
                    act.wait_ge(out_transposed, m + 1)
                    wait(act, out_squared, m - 1)
                    nc.scalar.activation(square_out[:, m % 2, :], psum[:, m % 8, :], ACT.Square,
                                         accum_out=stats[:, t, half:half + 1]).then_inc(out_squared, 1)
                act.wait_ge(out_total, t + 1)
                nc.scalar.activation(stats[:, t, 3:4], stats[:, t, 2:3], ACT.Sqrt, scale=1.0 / D_MODEL,
                                     bias=eps[:, 0:1]).then_inc(out_root, 1)

        @block.vector
        def _(dve):
            nc.vector.memset(eps[:], EPS).then_inc(eps_set, 1)
            for t in range(META_TILE + 1):
                cols = META if t == META_TILE else P
                dve.wait_ge(x_transposed, t + 1)
                src = psum[:, (2 * t) % 8, :].rearrange("p (k c) -> p k c", k=4)[:, :, 0:cols]
                nc.vector.tensor_copy(h[:, 0:4, t * P:t * P + cols], src).then_inc(h_low, 1)

            def norm(n, chunks):
                s = norms[n]

                def lo(c, kt):
                    m, (at, cols) = c * KT + kt, chunks[c]
                    dve.wait_ge(s["hi"], m + 1)
                    nc.vector.tensor_tensor(u_lo[:, kt, at:at + cols], un[:, m % 3, 0:cols],
                                            u_hi[:, kt, at:at + cols].bitcast(F32), ALU.subtract)\
                        .then_inc(s["lo"], 1)

                for c, (at, cols) in enumerate(chunks):
                    dve.wait_ge(s["root"], c + 1)
                    nc.vector.reciprocal(rstd[:, c % 2, 0:cols], rstd[:, c % 2, 0:cols]).then_inc(s["rstd"], 1)
                    dve.wait_ge(s["rstd"], c + 1)
                    for kt in range(KT):
                        m = c * KT + kt
                        wait(dve, s["lo"], m - 2)
                        nc.vector.scalar_tensor_tensor(out=un[:, m % 3, 0:cols], in0=h[:, kt, at:at + cols],
                                                       scalar=gains[:, n, kt:kt + 1], in1=rstd[:, c % 2, 0:cols],
                                                       op0=ALU.mult, op1=ALU.mult).then_inc(s["un"], 1)
                        if kt:
                            lo(c, kt - 1)
                    lo(c, KT - 1)
                norm_over(dve, n)

            def ffn(n, chunks):
                s = ffns[n]
                per_turn, adds = 2 * len(chunks), KT * len(chunks)
                with dve.Fori(0, FF_PAIRS) as i:
                    for c, (at, cols) in enumerate(chunks):
                        for ft in range(2):
                            m = 2 * c + ft
                            dve.wait_ge(s["silu"], per_turn * i + m + 1)
                            dve.wait_ge(s["up"], per_turn * i + m + 1)
                            if m >= 2:
                                dve.wait_ge(s["hid_lo"], per_turn * i + m - 1)
                            nc.vector.tensor_tensor(hidden[:, m % 2, 0:cols], silu_g[:, m % 2, 0:cols],
                                                    psum[:, 2 * (m % 2) + 1, 0:cols], ALU.mult)\
                                .then_inc(s["hidden"], 1)
                            dve.wait_ge(s["hid_hi"], per_turn * i + m + 1)
                            nc.vector.tensor_tensor(hid_lo[:, ft, at:at + cols], hidden[:, m % 2, 0:cols],
                                                    hid_hi[:, ft, at:at + cols].bitcast(F32), ALU.subtract)\
                                .then_inc(s["hid_lo"], 1)
                    for c, (at, cols) in enumerate(chunks):
                        for dt in range(KT):
                            m = c * KT + dt
                            dve.wait_ge(s["down"], adds * i + m + 1)
                            nc.vector.scalar_tensor_tensor(out=h[:, dt, at:at + cols], in0=psum[:, 4 + m % 4, 0:cols],
                                                           scalar=0.5, in1=h[:, dt, at:at + cols],
                                                           op0=ALU.mult, op1=ALU.add).then_inc(s["added"], 1)

            def head(hd, first):
                base = group_base(hd)

                def group_ready(g):
                    dve.wait_ge(grouped, base + g + 1)

                def lo(dst, src, hi, scale=None):
                    if scale is None:
                        done = nc.vector.tensor_tensor(dst, src, hi.bitcast(F32), ALU.subtract)
                    else:
                        done = nc.vector.scalar_tensor_tensor(out=dst, in0=src, scalar=scale, in1=hi.bitcast(F32),
                                                              op0=ALU.mult, op1=ALU.subtract)
                    done.then_inc(evacuated, 1)

                for c, (at, cols) in enumerate(ALL_CHUNKS):
                    group_ready(G_V + c)
                    nc.vector.tensor_copy(v_t[:, at:at + cols], psum[:, 6 + (G_V + c) % 2, 0:cols])\
                        .then_inc(evacuated, 1)
                dve.wait_ge(proj_hi, 8 * hd + 1)
                lo(q[:, 1, BANK:], psum[:, 6 + G_Q1 % 2, :], q[:, 0, BANK:], Q_SCALE)
                for c, (at, cols) in enumerate(ALL_CHUNKS):
                    dve.wait_ge(proj_hi, 8 * hd + 2 + c)
                    lo(k[:, 1, at:at + cols], psum[:, 6 + (G_K + c) % 2, 0:cols], k[:, 0, at:at + cols])
                for c, (t0, t1) in enumerate(VT_GROUPS):
                    rows = META if t0 == META_TILE else P
                    dve.wait_ge(proj_hi, 8 * hd + 5 + c)
                    src = psum[0:rows, 6 + (G_VT + c) % 2, 0:(t1 - t0) * P].rearrange("p (t d) -> p t d", d=P)
                    lo(v[0:rows, 1, t0:t1, :], src, v[0:rows, 0, t0:t1, :])
                for s in range(SLOTS):
                    if 2 <= s < S + 2:
                        t = s - 2
                        chunk, tile, at, n, _ = STEPS[t]
                        rows = META if tile == META_TILE else P
                        at -= chunk * BANK
                        dve.wait_ge(summed, S * hd + t + 1)
                        nc.vector.tensor_tensor(zs[0:rows, t % 4, 0:n], zs[0:rows, t % 4, 0:n],
                                                psum[0:rows, 2 + chunk, at:at + n], ALU.subtract)\
                            .then_inc(logw_done, 1)
                    if s < S:
                        n, rows = STEPS[s][3], META if STEPS[s][1] == META_TILE else P
                        e = sp[0:rows, s % 3, 0:n]
                        dve.wait_ge(logged, S * hd + s + 1)
                        nc.vector.scalar_tensor_tensor(out=e, in0=zs[0:rows, s % 4, 0:n], scalar=0.0, in1=e,
                                                       op0=ALU.max, op1=ALU.add).then_inc(softplused, 1)
                        dve.wait_ge(softplused, S * hd + s + 1)
                        if s >= 2 and STEPS[s - 2][1] == META_TILE:
                            dve.wait_ge(summed, S * hd + s - 1)
                        elif s >= 2:
                            dve.wait_ge(completed, COMPLETIONS * hd + completions_before(s - 1))
                        nc.vector.tensor_copy(sp_hi[0:rows, s % 2, 0:n], e).then_inc(sp_hi_done, 1)
                    if 2 <= s < S + 2:
                        t = s - 2
                        n, rows = STEPS[t][3], META if STEPS[t][1] == META_TILE else P
                        dve.wait_ge(w_done, S * hd + t + 1)
                        wait(dve, weighed, S * hd + (t - 1 if t >= 2 else 0))
                        nc.vector.tensor_copy(w_hi[0:rows, t % 2, 0:n], wf[0:rows, t % 2, 0:n])\
                            .then_inc(w_hi_done, 1)
                    if s == Q0_SLOTS - 1:
                        dve.wait_ge(proj_hi, 8 * hd + 8)
                        lo(q[:, 1, 0:BANK], psum[:, 6 + G_Q0 % 2, :], q[:, 0, 0:BANK], Q_SCALE)
                    for place in (0, 1):
                        if not first:
                            for g in o_groups(s, place):
                                group_ready(G_O + g)
                                add_output(g)
                    for chunk, slot in ((1, LAST_OF_CHUNK[1] + 4), (0, SLOTS - 1)):
                        if s == slot:
                            cols = slice(chunk * BANK, (chunk + 1) * BANK)
                            dve.wait_ge(o_hi_done, 2 * hd + 2 - chunk)
                            nc.vector.tensor_tensor(o[:, 1, cols], psum[:, 4 + chunk, :], o[:, 0, cols].bitcast(F32),
                                                    ALU.subtract).then_inc(o_lo_done, 1)

            def add_output(g):
                dt, chunk = g % KT, 1 - g // KT
                cols = slice(chunk * BANK, (chunk + 1) * BANK)
                nc.vector.tensor_tensor(h[:, dt, cols], psum[:, 6 + (G_O + g) % 2, :], h[:, dt, cols], ALU.add)\
                    .then_inc(evacuated, 1)

            dve.wait_ge(gains_loaded, 16)
            dve.wait_ge(h_low, META_TILE + 1)
            dve.wait_ge(h_high, META_TILE + 1)
            norm(0, ALL_CHUNKS)
            ffn(0, ALL_CHUNKS)
            ffn_over(dve, 0)
            norm(1, ALL_CHUNKS)
            head(0, first=True)
            with dve.Fori(1, HEADS) as hd:
                head(hd, first=False)
            for g in range(16):
                dve.wait_ge(grouped, group_base(HEADS) + g + 1)
                add_output(g)
            attention_over(dve)
            norm(2, FRAME_CHUNKS)
            ffn(1, FRAME_CHUNKS)

            dve.wait_ge(gain_loaded, 16)

            def scale_rows(t):
                if t >= 4:
                    dve.wait_ge(out_stored[t % 4], 16 * (t // 4))
                dve.wait_ge(out_rstd, t + 1)
                for half in range(2):
                    cols = slice(half * BANK, (half + 1) * BANK)
                    nc.vector.scalar_tensor_tensor(out=out_tiles[:, t % 4, cols], in0=psum[:, (2 * t + half) % 8, :],
                                                   scalar=stats[:, t, 3:4], in1=gain_row[:, cols],
                                                   op0=ALU.mult, op1=ALU.mult).then_inc(out_scaled, 1)

            for t in range(FRAMES // P):
                dve.wait_ge(out_squared, 2 * t + 2)
                nc.vector.tensor_tensor(stats[:, t, 2:3], stats[:, t, 0:1], stats[:, t, 1:2], ALU.add)\
                    .then_inc(out_total, 1)
                if t:
                    scale_rows(t - 1)
                dve.wait_ge(out_root, t + 1)
                nc.vector.reciprocal(stats[:, t, 3:4], stats[:, t, 3:4]).then_inc(out_rstd, 1)
            scale_rows(FRAMES // P - 1)

        @block.tensor
        def _(pe):
            def product(dst, w_halves, x_halves, start, stop):
                (wh, wl), (xh, xl) = w_halves, x_halves
                nc.tensor.matmul(dst, wh, xh, start=start, stop=False, skip_group_check=True)
                nc.tensor.matmul(dst, wh, xl, start=False, stop=False, skip_group_check=True)
                return nc.tensor.matmul(dst, wl, xh, start=False, stop=stop, skip_group_check=True)

            pe.wait_ge(const_set, CONSTANTS)
            for t in range(META_TILE + 1):
                rows = META if t == META_TILE else P
                pe.wait_ge(x_loaded[t % 4], 16 * (t // 4 + 1))
                if t >= 4:
                    pe.wait_ge(h_low, t - 3)
                    pe.wait_ge(h_high, t - 3)
                for kt in range(KT):
                    dst = psum[:, (2 * t + kt // 4) % 8, (kt % 4) * P:(kt % 4) * P + rows]
                    last = nc.tensor.transpose(dst, x_tiles[0:rows, t % 4, kt * P:(kt + 1) * P],
                                               ident[0:rows, 0:rows])
                last.then_inc(x_transposed, 1)

            def norm(n, chunks):
                s = norms[n]
                for c, (_, cols) in enumerate(chunks):
                    for kt in range(KT):
                        m = c * KT + kt
                        pe.wait_ge(s["squared"], m + 1)
                        nc.tensor.matmul(psum[:, NORM_BANK + c, 0:cols], ones[:], sq[:, m % 3, 0:cols],
                                         start=kt == 0, stop=kt == KT - 1).then_inc(s["summed"], 1)

            def ffn(n, chunks):
                s = ffns[n]
                per_turn, adds = 2 * len(chunks), KT * len(chunks)
                with pe.Fori(0, FF_PAIRS) as i:
                    for c, (at, cols) in enumerate(chunks):
                        pe.wait_ge(norms[n * 2]["lo"], KT * (c + 1))
                        for ft in range(2):
                            m = 2 * c + ft
                            if m >= 2:
                                pe.wait_ge(s["hidden"], per_turn * i + m - 1)
                            for w, split, done, bank in ((wg, "g_split", "gate", 0), (wu, "u_split", "up", 1)):
                                if m == 0:
                                    pe.wait_ge(s[split], i + 1)
                                f = slice(ft * P, (ft + 1) * P)
                                for kt in range(KT):
                                    last = product(psum[:, 2 * (m % 2) + bank, 0:cols],
                                                   (w[:, 0, kt, f], w[:, 1, kt, f]),
                                                   (u_hi[:, kt, at:at + cols], u_lo[:, kt, at:at + cols]),
                                                   start=kt == 0, stop=kt == KT - 1)
                                last.then_inc(s[done], 1)
                    pe.wait_ge(s["d_split"], i + 1)
                    for c, (at, cols) in enumerate(chunks):
                        pe.wait_ge(s["hid_lo"], per_turn * i + 2 * c + 2)
                        for dt in range(KT):
                            m = c * KT + dt
                            if m >= 4:
                                pe.wait_ge(s["added"], adds * i + m - 3)
                            d = slice(dt * P, (dt + 1) * P)
                            for ft in range(2):
                                last = product(psum[:, 4 + m % 4, 0:cols], (wd[:, 0, ft, d], wd[:, 1, ft, d]),
                                               (hid_hi[:, ft, at:at + cols], hid_lo[:, ft, at:at + cols]),
                                               start=ft == 0, stop=ft == 1)
                            last.then_inc(s["down"], 1)

            def output_group(g):
                dt, chunk = g % KT, 1 - g // KT
                cols, d = slice(chunk * BANK, (chunk + 1) * BANK), slice(dt * P, (dt + 1) * P)
                product(psum[:, 6 + (G_O + g) % 2, :], (wo[:, 0, d], wo[:, 1, d]),
                        (o[:, 0, cols], o[:, 1, cols]), start=True, stop=True).then_inc(grouped, 1)

            def head(hd, first):
                base = group_base(hd)

                def bank_free(g):
                    wait(pe, evacuated, base + (g - 1 if g else 0))

                def project(g, w, at, cols, kts=range(KT)):
                    for kt in kts:
                        last = product(psum[:, 6 + g % 2, 0:cols], (w[:, 0, kt, :], w[:, 1, kt, :]),
                                       (u_hi[:, kt, at:at + cols], u_lo[:, kt, at:at + cols]),
                                       start=kt == 0, stop=kt == KT - 1)
                    if kts[-1] == KT - 1:
                        last.then_inc(grouped, 1)

                units = 4 * hd
                pe.wait_ge(a_split, units if not first else 1)
                for c, (at, cols) in enumerate(ALL_CHUNKS):
                    pe.wait_ge(norms[1]["lo"], KT * (c + 1))
                    bank_free(G_V + c)
                    project(G_V + c, w_kv, at, cols)
                bank_free(G_Q1)
                pe.wait_ge(a_split, units + 1 if not first else 2)
                project(G_Q1, wq, BANK, BANK)
                pe.wait_ge(a_split, units + 3)
                for c, (at, cols) in enumerate(ALL_CHUNKS):
                    bank_free(G_K + c)
                    project(G_K + c, w_kv, at, cols)
                for c, (t0, t1) in enumerate(VT_GROUPS):
                    bank_free(G_VT + c)
                    if c == 0:
                        pe.wait_ge(evacuated, base + 3)
                    for t in range(t0, t1):
                        rows = META if t == META_TILE else P
                        dst = psum[0:rows, 6 + (G_VT + c) % 2, (t - t0) * P:(t - t0 + 1) * P]
                        last = nc.tensor.transpose(dst, v_t[:, t * P:t * P + rows], ident[:])
                    last.then_inc(grouped, 1)

                def score(t):
                    _, tile, at, n, mask_at = STEPS[t]
                    rows = META if tile == META_TILE else P
                    keys = slice(tile * P, tile * P + rows)
                    if t == 0:
                        pe.wait_ge(evacuated, base + G_VT)
                    if t == LAST_OF_CHUNK[1] + 1:
                        pe.wait_ge(evacuated, base + G_Q0 + 1)
                    if t >= 2:
                        pe.wait_ge(z_read, 2 * (S * hd + t - 1))
                    dst = psum[0:rows, t % 2, 0:n]
                    last = product(dst, (k[:, 0, keys], k[:, 1, keys]), (q[:, 0, at:at + n], q[:, 1, at:at + n]),
                                   start=True, stop=mask_at is None)
                    if mask_at is not None:
                        last = nc.tensor.matmul(psum[:, t % 2, 0:2 * P], ident_r[:], mask[:, mask_at:mask_at + 2 * P],
                                                start=False, stop=True, skip_group_check=True)
                    last.then_inc(scored, 1)

                def running_sum(t, triangle, start, stop):
                    chunk, tile, at, n, _ = STEPS[t]
                    rows = META if tile == META_TILE else P
                    at -= chunk * BANK
                    dst = psum[:, 2 + chunk, at:at + n]
                    nc.tensor.matmul(dst, triangle[0:rows, :], sp_hi[0:rows, t % 2, 0:n],
                                     start=start, stop=False, skip_group_check=True)
                    return nc.tensor.matmul(dst, triangle[0:rows, :], sp_lo[0:rows, t % 2, 0:n],
                                            start=False, stop=stop, skip_group_check=True)

                def weigh(t):
                    chunk, tile, at, n, _ = STEPS[t]
                    rows = META if tile == META_TILE else P
                    at -= chunk * BANK
                    start = t == 0 or STEPS[t - 1][0] != chunk
                    if t == 0:
                        pe.wait_ge(evacuated, base + G_Q0)
                    if start:
                        wait(pe, o_lo_done, 2 * hd - chunk)
                    pe.wait_ge(w_lo_done, S * hd + t + 1)
                    product(psum[:, 4 + chunk, at:at + n], (v[0:rows, 0, tile, :], v[0:rows, 1, tile, :]),
                            (w_hi[0:rows, t % 2, 0:n], w_lo[0:rows, t % 2, 0:n]),
                            start=start, stop=tile == META_TILE).then_inc(weighed, 1)

                def other(s, place):
                    if s < Q0_SLOTS:
                        kt = 2 * s + place
                        if kt == 0:
                            bank_free(G_Q0)
                        project(G_Q0, wq, 0, BANK, range(kt, kt + 1))
                    if first:
                        return
                    for g in o_groups(s, place):
                        if g == 0:
                            pe.wait_ge(a_split, units + 2)
                            pe.wait_ge(o_lo_done, 2 * hd)
                        bank_free(G_O + g)
                        output_group(g)

                for s in range(SLOTS):
                    if s < S:
                        score(s)
                    other(s, 0)
                    t = s - 2
                    if 0 <= t < S:
                        start = t == 0 or STEPS[t - 1][0] != STEPS[t][0]
                        pe.wait_ge(sp_lo_done, S * hd + t + 1)
                        running_sum(t, tri, start, STEPS[t][1] == META_TILE).then_inc(summed, 1)
                    other(s, 1)
                    if 0 <= t < S and STEPS[t][1] != META_TILE:
                        pe.wait_ge(logw_done, S * hd + t + 1)
                        running_sum(t, tri_rest, False, False).then_inc(completed, 1)
                    if 0 <= s - 3 < S:
                        weigh(s - 3)

            norm(0, ALL_CHUNKS)
            ffn(0, ALL_CHUNKS)
            norm(1, ALL_CHUNKS)
            head(0, first=True)
            with pe.Fori(1, HEADS) as hd:
                head(hd, first=False)
            pe.wait_ge(a_split, 4 * HEADS)
            pe.wait_ge(o_lo_done, 2 * HEADS)
            for g in range(16):
                wait(pe, evacuated, group_base(HEADS) + (g - 1 if g else 0))
                output_group(g)
            norm(2, FRAME_CHUNKS)
            ffn(1, FRAME_CHUNKS)

            ffn_over(pe, 1)
            for t in range(FRAMES // P):
                if t >= 4:
                    pe.wait_ge(out_scaled, 2 * (t - 3))
                for kt in range(KT):
                    last = nc.tensor.transpose(psum[:, (2 * t + kt // 4) % 8, (kt % 4) * P:(kt % 4 + 1) * P],
                                               h[:, kt, t * P:(t + 1) * P], ident[:])
                    if kt % 4 == 3:
                        last.then_inc(out_transposed, 1)


def kernel(**inputs):
    import numpy as np
    import concourse.bacc as bacc
    from concourse.bass_utils import run_bass_kernel_spmd

    nc = bacc.Bacc("TRN2", target_bir_lowering=False, num_devices=1)
    gains = np.stack([np.asarray(inputs[name][0]).reshape(KT, P).T for name in ("ffn1_norm", "mix_norm", "ffn2_norm")],
                     axis=1)
    arrays = {
        "x": inputs["x"][0], "meta": inputs["meta_tokens"],
        "gains": gains, "w1_in": inputs["ffn1_w_in"][0], "w1_out": inputs["ffn1_w_out"][0],
        "w2_in": inputs["ffn2_w_in"][0], "w2_out": inputs["ffn2_w_out"][0],
        "w_qkv": inputs["sb_w_qkv"][0], "w_o": inputs["sb_w_o"][0], "g_final": inputs["final_norm"],
    }
    arrays = {name + "_dram": np.ascontiguousarray(a) for name, a in arrays.items()}
    args = [nc.dram_tensor(name, a.shape, mybir.dt.from_np(a.dtype), kind="ExternalInput").ap()
            for name, a in arrays.items()]
    out = nc.dram_tensor("out_dram", (FRAMES, D_MODEL), F32, kind="ExternalOutput").ap()
    build(nc, *args, out)
    r = run_bass_kernel_spmd(nc, [arrays], core_ids=[0])
    return r.results[0]["out_dram"].reshape(1, FRAMES, D_MODEL)
```

```python
from contextlib import ExitStack

import concourse.bass as bass
from concourse import mybir

F32 = mybir.dt.float32
F32R = mybir.dt.float32r
ALU = mybir.AluOpType
ACT = mybir.ActivationFunctionType

P = 128
BANK = 512
FRAMES, META, D_MODEL = 1024, 16, 1024
TOKENS = FRAMES + META
KT = D_MODEL // P
D_FF = 2816
FF_PAIRS = D_FF // (2 * P)
HEADS = 8
EPS = 1e-5
Q_SCALE = float(P) ** -0.5
NEG = -1e30

ALL_CHUNKS = [(0, 348), (348, 348), (696, 344)]
FRAME_CHUNKS = [(0, BANK), (BANK, BANK)]

META_TILE = FRAMES // P

X_TILES = [range(0, 3), range(3, 6), range(6, META_TILE + 1)]


def attention_steps():
    steps = []
    for chunk in (1, 0):
        q_begin, q_end = chunk * BANK, (chunk + 1) * BANK
        for tile in range(q_end // P - 1, -1, -1):
            first = min(max(tile * P, q_begin), q_end - 2 * P)
            mask = None if tile * P < q_begin else P - (tile * P - first)
            steps.append((chunk, tile, first, q_end - first, mask))
        steps.append((chunk, META_TILE, q_begin, BANK, None))
    return steps


STEPS = attention_steps()
S = len(STEPS)
COMPLETIONS = sum(tile != META_TILE for _, tile, _, _, _ in STEPS)
LAST_OF_CHUNK = {chunk: max(t for t in range(S) if STEPS[t][0] == chunk) for chunk in (0, 1)}
SLOTS = S + 4

G_Q1, G_VT, G_K, G_O = 0, 1, 4, 7
K_ORDER = (2, 1, 0)
O_GROUPS, V_GROUPS = 16, 3
LAST_O_ORDER = [*range(KT, 2 * KT), *range(KT)]
Q1_BANK, VT_BANKS, K_BANKS, V_BANKS = 7, (0, 1, 2), (6, 7, 3), (6, 7, 6)
Q0_BANK, O_BANK = 6, 7
VT_GROUPS = [(0, 4), (4, 8), (8, 9)]
V_FIRST_SLOT = KT + 1
V_SLOT = V_FIRST_SLOT + KT
OLD_GROUPS = V_GROUPS + G_O + V_GROUPS
GROUPS = G_O + O_GROUPS + V_GROUPS


def first_v_group(first):
    return G_O if first else G_O + O_GROUPS


def group_base(h):
    return V_GROUPS if isinstance(h, int) and h == 0 else GROUPS * h - (GROUPS - OLD_GROUPS)


GROUPS_BEFORE_LAST_O = GROUPS * HEADS - (GROUPS - OLD_GROUPS) - V_GROUPS


def completions_before(t):
    return sum(STEPS[s][1] != META_TILE for s in range(t))


def wait(engine, semaphore, value):
    if isinstance(value, int) and value <= 0:
        return
    engine.wait_ge(semaphore, value)


def build(nc, x, meta, gains_in, w1_in, w1_out, w2_in, w2_out, w_qkv, w_o, g_final, out):
    ctx = ExitStack()
    with ctx:
        def sbuf(name, shape, dtype):
            return ctx.enter_context(nc.sbuf_tensor(name, shape, dtype))

        def sem(name):
            return ctx.enter_context(nc.semaphore(name))

        h = sbuf("h", [P, KT, TOKENS], F32)
        u_hi = sbuf("u_hi", [P, KT, TOKENS], F32R)
        u_lo = sbuf("u_lo", [P, KT, TOKENS], F32R)
        scratch = sbuf("scratch", [P, 8192], F32)
        work = sbuf("work", [P, 18720], F32R)
        tri = sbuf("tri", [P, P], F32R)
        tri_rest = sbuf("tri_rest", [P, P], F32R)
        ident_r = sbuf("ident_r", [P, P], F32R)
        mask = sbuf("mask", [P, 3 * P], F32R)
        ident = sbuf("ident", [P, P], F32)
        ones = sbuf("ones", [P, P], F32)
        gains = sbuf("gains", [P, 3, KT], F32)
        stats = sbuf("stats", [P, KT, 4], F32)
        eps = sbuf("eps", [P, 1], F32)
        psum = ctx.enter_context(nc.psum_tensor("psum", [P, 8, BANK], F32))

        def piece(arena, at, *dims):
            size = 1
            for n in dims:
                size *= n
            flat = arena[:, at:at + size]
            if len(dims) == 2:
                return flat.rearrange("p (a b) -> p a b", a=dims[0])
            if len(dims) == 3:
                return flat.rearrange("p (a b c) -> p a b c", a=dims[0], b=dims[1])
            return flat

        x_tiles = piece(scratch, 0, 4, D_MODEL)
        sq = piece(scratch, 4096, 3, BANK)
        rstd = piece(scratch, 5632, 2, BANK)
        un = piece(scratch, 6656, 3, BANK)
        stage_g = piece(scratch, 0, KT, 2 * P)
        stage_u = piece(scratch, 2048, KT, 2 * P)
        stage_d = piece(scratch, 4096, 2, D_MODEL)
        silu_g = piece(scratch, 6144, 2, BANK)
        hidden = piece(scratch, 7168, 2, BANK)
        stage_a = piece(scratch, 0, 2, D_MODEL)
        zs = piece(scratch, 2048, 4, BANK)
        sp = piece(scratch, 4096, 3, BANK)
        wf = piece(scratch, 5632, 2, BANK)
        v_t = piece(scratch, 6656, TOKENS)
        out_tiles = piece(scratch, 0, 4, D_MODEL)
        gain_row = piece(scratch, 4096, D_MODEL)
        square_out = piece(scratch, 6144, 2, BANK)

        wg = piece(work, 0, 2, KT, 2 * P)
        wu = piece(work, 4096, 2, KT, 2 * P)
        wd = piece(work, 8192, 2, 2, D_MODEL)
        hid_hi = piece(work, 12288, 2, TOKENS)
        hid_lo = piece(work, 14368, 2, TOKENS)
        wq = piece(work, 0, 2, KT, P)
        w_kv = piece(work, 2048, 2, KT, P)
        wo = piece(work, 4096, 2, D_MODEL)
        q = piece(work, 6144, 2, FRAMES)
        k = piece(work, 8192, 2, TOKENS)
        v = piece(work, 10272, 2, META_TILE + 1, P)
        o = piece(work, 12576, 2, FRAMES)
        sp_hi = piece(work, 14624, 2, BANK)
        sp_lo = piece(work, 15648, 2, BANK)
        w_hi = piece(work, 16672, 2, BANK)
        w_lo = piece(work, 17696, 2, BANK)

        const_set = sem("const_set")
        gains_loaded = sem("gains_loaded")
        x_loaded = [sem(f"x_loaded{i}") for i in range(4)]
        x_transposed = sem("x_transposed")
        h_low = sem("h_low")
        h_high = sem("h_high")
        norms = [{name: sem(f"norm{n}_{name}") for name in
                  ("squared", "summed", "root", "rstd", "un", "hi", "lo")} for n in range(3)]
        ffns = [{name: sem(f"ffn{n}_{name}") for name in
                 ("g_loaded", "u_loaded", "d_loaded", "g_hi", "u_hi", "d_hi", "g_split", "u_split",
                  "d_split", "gate", "up", "silu", "hidden", "hid_hi", "hid_lo", "down", "added")}
                for n in range(2)]
        a_loaded = [sem(f"a_loaded{i}") for i in range(2)]
        a_hi = sem("a_hi")
        a_split = sem("a_split")
        grouped = sem("grouped")
        evacuated = sem("evacuated")
        q0_grouped = sem("q0_grouped")
        q0_evacuated = sem("q0_evacuated")
        proj_hi = sem("proj_hi")
        scored = sem("scored")
        z_read = sem("z_read")
        eps_set = sem("eps_set")
        exped = sem("exped")
        logged = sem("logged")
        softplused = sem("softplused")
        sp_hi_done = sem("sp_hi_done")
        sp_lo_done = sem("sp_lo_done")
        summed = sem("summed")
        completed = sem("completed")
        logw_done = sem("logw_done")
        w_done = sem("w_done")
        w_hi_done = sem("w_hi_done")
        w_lo_done = sem("w_lo_done")
        weighed = sem("weighed")
        o_hi_done = sem("o_hi_done")
        o_lo_done = sem("o_lo_done")
        gain_loaded = sem("gain_loaded")
        out_transposed = sem("out_transposed")
        out_squared = sem("out_squared")
        out_total = sem("out_total")
        out_root = sem("out_root")
        out_rstd = sem("out_rstd")
        out_scaled = sem("out_scaled")
        out_stored = [sem(f"out_stored{i}") for i in range(4)]

        CONSTANTS = 8
        NORM_BANKS = (3, 0, 3)

        def attention_over(engine):
            engine.wait_ge(evacuated, GROUPS_BEFORE_LAST_O + O_GROUPS)

        def ffn_over(engine, n):
            chunks = len(ALL_CHUNKS) if n == 0 else len(FRAME_CHUNKS)
            engine.wait_ge(ffns[n]["added"], FF_PAIRS * chunks * KT)

        def norm_over(engine, n):
            engine.wait_ge(norms[n]["lo"], KT * (len(FRAME_CHUNKS) if n == 2 else len(ALL_CHUNKS)))

        block = ctx.enter_context(nc.Block())

        @block.sync
        def _(sp_eng):
            def load_x(t):
                rows = META if t == META_TILE else P
                src = meta[:, :] if t == META_TILE else x[t * P:(t + 1) * P, :]
                if t >= 4:
                    sp_eng.wait_ge(x_transposed, t - 3)
                sp_eng.dma_start(x_tiles[0:rows, t % 4, :], src).then_inc(x_loaded[t % 4], 16)

            def ffn_sources(n, i):
                w_in, w_out = (w1_in, w1_out) if n == 0 else (w2_in, w2_out)
                gate = w_in[:, bass.ds(i * (2 * P), 2 * P)].rearrange("(k p) f -> p k f", p=P)
                up = w_in[:, bass.ds((i + FF_PAIRS) * (2 * P), 2 * P)].rearrange("(k p) f -> p k f", p=P)
                down = w_out[bass.ds(i * (2 * P), 2 * P), :].rearrange("(t p) d -> p t d", p=P)
                return gate, up, down

            def ffn_rest(n):
                s = ffns[n]
                with sp_eng.Fori(1, FF_PAIRS) as i:
                    gate, up, down = ffn_sources(n, i)
                    sp_eng.wait_ge(s["g_split"], i)
                    sp_eng.dma_start(stage_g, gate).then_inc(s["g_loaded"], 16)
                    sp_eng.wait_ge(s["u_split"], i)
                    sp_eng.dma_start(stage_u, up).then_inc(s["u_loaded"], 16)
                    sp_eng.wait_ge(s["d_split"], i)
                    sp_eng.dma_start(stage_d, down).then_inc(s["d_loaded"], 16)

            load_x(0)
            sp_eng.dma_start(gains[:], gains_in[:, :, :]).then_inc(gains_loaded, 16)
            for t in range(1, META_TILE + 1):
                load_x(t)
            gate, up, down = ffn_sources(0, 0)
            sp_eng.wait_ge(x_transposed, META_TILE + 1)
            sp_eng.dma_start(stage_g, gate).then_inc(ffns[0]["g_loaded"], 16)
            sp_eng.dma_start(stage_u, up).then_inc(ffns[0]["u_loaded"], 16)
            sp_eng.wait_ge(norms[0]["lo"], len(ALL_CHUNKS) * KT)
            sp_eng.dma_start(stage_d, down).then_inc(ffns[0]["d_loaded"], 16)
            ffn_rest(0)

            def load_a(unit, kind, head):
                slot = unit[0] % 2
                if kind == 3:
                    src = w_o[bass.ds(head * P, P), :]
                else:
                    src = w_qkv[:, bass.ds((head + kind * HEADS) * P, P)].rearrange("(k p) f -> p k f", p=P)
                dst = stage_a[:, slot, :]
                if kind != 3:
                    dst = dst.rearrange("p (k f) -> p k f", k=KT)
                wait(sp_eng, a_split, unit[0] - 1 + 4 * unit[1])
                sp_eng.dma_start(dst, src).then_inc(a_loaded[slot], 16)

            sp_eng.wait_ge(ffns[0]["g_split"], FF_PAIRS)
            load_a((0, 0), 2, 0)
            load_a((1, 0), 0, 0)
            load_a((2, 0), 1, 0)
            with sp_eng.Fori(0, HEADS - 1) as hd:
                load_a((3, hd), 2, hd + 1)
                load_a((4, hd), 0, hd + 1)
                load_a((5, hd), 3, hd)
                load_a((6, hd), 1, hd + 1)
            load_a((3, HEADS - 1), 3, HEADS - 1)

            gate, up, down = ffn_sources(1, 0)
            sp_eng.wait_ge(a_split, 4 * HEADS)
            sp_eng.dma_start(stage_g, gate).then_inc(ffns[1]["g_loaded"], 16)
            sp_eng.wait_ge(evacuated, GROUPS_BEFORE_LAST_O + 1)
            sp_eng.dma_start(stage_u, up).then_inc(ffns[1]["u_loaded"], 16)
            sp_eng.wait_ge(norms[2]["lo"], len(FRAME_CHUNKS) * KT)
            sp_eng.dma_start(stage_d, down).then_inc(ffns[1]["d_loaded"], 16)
            ffn_rest(1)

            sp_eng.wait_ge(ffns[1]["d_split"], FF_PAIRS)
            sp_eng.dma_start(gain_row, g_final.rearrange("(a n) -> a n", a=1).to_broadcast([P, D_MODEL]))\
                .then_inc(gain_loaded, 16)
            for t in range(FRAMES // P):
                sp_eng.wait_ge(out_scaled, 2 * (t + 1))
                sp_eng.dma_start(out[t * P:(t + 1) * P, :], out_tiles[:, t % 4, :]).then_inc(out_stored[t % 4], 16)
            for slot in range(4):
                sp_eng.wait_ge(out_stored[slot], 16 * (FRAMES // P // 4))

        @block.gpsimd
        def _(pool):
            nc.gpsimd.memset(ident[:], 0.0).then_inc(const_set, 1)
            nc.gpsimd.memset(ones[:], 1.0).then_inc(const_set, 1)
            nc.gpsimd.memset(h[:, 0, 0:3 * P], 0.0).then_inc(const_set, 1)
            pool.wait_ge(const_set, 3)
            nc.gpsimd.affine_select(out=ident[:], in_=ident[:], compare_op=ALU.not_equal, fill=1.0, base=0,
                                    pattern=[[-1, P]], channel_multiplier=1).then_inc(const_set, 1)
            nc.gpsimd.affine_select(out=tri[:], in_=ones[:], compare_op=ALU.is_ge, fill=0.0, base=0,
                                    pattern=[[-1, P]], channel_multiplier=1).then_inc(const_set, 1)
            nc.gpsimd.affine_select(out=tri_rest[:], in_=ones[:], compare_op=ALU.is_gt, fill=0.0, base=0,
                                    pattern=[[1, P]], channel_multiplier=-1).then_inc(const_set, 1)
            nc.gpsimd.affine_select(out=mask[:], in_=h[:, 0, 0:3 * P], compare_op=ALU.is_gt, fill=NEG, base=-P,
                                    pattern=[[1, 3 * P]], channel_multiplier=-1).then_inc(const_set, 1)
            pool.wait_ge(const_set, 4)
            nc.gpsimd.tensor_copy(ident_r[:], ident[:]).then_inc(const_set, 1)

            def ffn(n):
                s = ffns[n]

                def split_gate_up(turn):
                    pool.wait_ge(s["g_hi"], turn + 1)
                    nc.gpsimd.tensor_tensor(wg[:, 1], stage_g, wg[:, 0].bitcast(F32), ALU.subtract)\
                        .then_inc(s["g_split"], 1)
                    pool.wait_ge(s["u_hi"], turn + 1)
                    nc.gpsimd.tensor_tensor(wu[:, 1], stage_u, wu[:, 0].bitcast(F32), ALU.subtract)\
                        .then_inc(s["u_split"], 1)

                def split_down(turn):
                    pool.wait_ge(s["d_hi"], turn + 1)
                    nc.gpsimd.tensor_tensor(wd[:, 1], stage_d, wd[:, 0].bitcast(F32), ALU.subtract)\
                        .then_inc(s["d_split"], 1)

                split_gate_up(0)
                with pool.Fori(0, FF_PAIRS - 1) as i:
                    split_down(i)
                    split_gate_up(i + 1)
                split_down(FF_PAIRS - 1)

            ffn(0)

            def split_weights(unit, kind):
                dst = (wq, w_kv, w_kv, wo)[kind]
                src = stage_a[:, unit[0] % 2, :]
                if kind != 3:
                    src = src.rearrange("p (k f) -> p k f", k=KT)
                pool.wait_ge(a_hi, unit[0] + 1 + 4 * unit[1])
                nc.gpsimd.tensor_tensor(dst[:, 1], src, dst[:, 0].bitcast(F32), ALU.subtract)\
                    .then_inc(a_split, 1)

            def head(hd, last):
                for s in range(SLOTS):
                    if s < S:
                        n, rows = STEPS[s][3], META if STEPS[s][1] == META_TILE else P
                        pool.wait_ge(sp_hi_done, S * hd + s + 1)
                        nc.gpsimd.tensor_tensor(sp_lo[0:rows, s % 2, 0:n], sp[0:rows, s % 3, 0:n],
                                                sp_hi[0:rows, s % 2, 0:n].bitcast(F32), ALU.subtract)\
                            .then_inc(sp_lo_done, 1)
                    if 2 <= s < S + 2:
                        t = s - 2
                        n, rows = STEPS[t][3], META if STEPS[t][1] == META_TILE else P
                        pool.wait_ge(w_hi_done, S * hd + t + 1)
                        nc.gpsimd.tensor_tensor(w_lo[0:rows, t % 2, 0:n], wf[0:rows, t % 2, 0:n],
                                                w_hi[0:rows, t % 2, 0:n].bitcast(F32), ALU.subtract)\
                            .then_inc(w_lo_done, 1)
                    if s == 5 and not last:
                        split_weights((3, hd), 2)
                    if s == 9 and not last:
                        split_weights((4, hd), 0)
                if last:
                    split_weights((3, hd), 3)
                else:
                    split_weights((5, hd), 3)
                    split_weights((6, hd), 1)

            split_weights((0, 0), 2)
            split_weights((1, 0), 0)
            split_weights((2, 0), 1)
            with pool.Fori(0, HEADS - 1) as hd:
                head(hd, last=False)
            head(HEADS - 1, last=True)

            ffn(1)

        @block.scalar
        def _(act):
            def take_high(c):
                for t in X_TILES[c]:
                    cols = META if t == META_TILE else P
                    act.wait_ge(x_transposed, t + 1)
                    src = psum[:, 6 * (t % 2) + 1, :].rearrange("p (k c) -> p k c", k=4)[:, :, 0:cols]
                    nc.scalar.activation(h[:, 4:8, t * P:t * P + cols], src, ACT.Copy).then_inc(h_high, 1)
                act.wait_ge(h_high, X_TILES[c][-1] + 1)
                act.wait_ge(h_low, X_TILES[c][-1] + 1)

            def norm(n, chunks, before_chunk, meanwhile):
                s = norms[n]

                def square(c, kt):
                    m, (at, cols) = c * KT + kt, chunks[c]
                    wait(act, s["summed"], m - 2)
                    nc.scalar.activation(sq[:, m % 3, 0:cols], h[:, kt, at:at + cols], ACT.Square)\
                        .then_inc(s["squared"], 1)

                def root(c):
                    cols = chunks[c][1]
                    act.wait_ge(s["summed"], KT * (c + 1))
                    if c >= 2:
                        act.wait_ge(s["un"], KT * (c - 1))
                    nc.scalar.activation(rstd[:, c % 2, 0:cols], psum[:, NORM_BANKS[n] + c, 0:cols], ACT.Sqrt,
                                         scale=1.0 / D_MODEL, bias=eps[:, 0:1]).then_inc(s["root"], 1)

                def hi(c, kt):
                    m, (at, cols) = c * KT + kt, chunks[c]
                    act.wait_ge(s["un"], m + 1)
                    nc.scalar.activation(u_hi[:, kt, at:at + cols], un[:, m % 3, 0:cols], ACT.Copy)\
                        .then_inc(s["hi"], 1)

                nc.scalar.preload_act_table(ACT.Sqrt)
                ahead = len(chunks) - 1
                for c in range(ahead):
                    before_chunk(c)
                    for kt in range(KT):
                        if n and c == 0 and kt == 3:
                            meanwhile()
                        square(c, kt)
                root(0)
                before_chunk(ahead)
                for kt in range(KT):
                    square(ahead, kt)
                    hi(0, kt)
                if not n:
                    meanwhile()
                for c in range(1, len(chunks)):
                    root(c)
                    for kt in range(KT):
                        hi(c, kt)
                norm_over(act, n)

            def split_gate_up(n, turn):
                s = ffns[n]
                act.wait_ge(s["g_loaded"], 16 * turn + 16)
                nc.scalar.activation(wg[:, 0], stage_g, ACT.Copy).then_inc(s["g_hi"], 1)
                act.wait_ge(s["u_loaded"], 16 * turn + 16)
                if n == 1 and isinstance(turn, int) and turn == 0:
                    attention_over(act)
                nc.scalar.activation(wu[:, 0], stage_u, ACT.Copy).then_inc(s["u_hi"], 1)

            def ffn(n, chunks):
                s = ffns[n]
                per_turn = 2 * len(chunks)

                def turn(i, last):
                    for c, (at, cols) in enumerate(chunks):
                        for ft in range(2):
                            m = 2 * c + ft
                            act.wait_ge(s["gate"], per_turn * i + m + 1)
                            nc.scalar.activation(silu_g[:, m % 2, 0:cols], psum[:, 2 * (m % 2), 0:cols], ACT.Silu)\
                                .then_inc(s["silu"], 1)
                            act.wait_ge(s["hidden"], per_turn * i + m + 1)
                            nc.scalar.activation(hid_hi[:, ft, at:at + cols], hidden[:, m % 2, 0:cols], ACT.Copy)\
                                .then_inc(s["hid_hi"], 1)
                            if m == 0:
                                act.wait_ge(s["d_loaded"], 16 * i + 16)
                                nc.scalar.activation(wd[:, 0], stage_d, ACT.Copy).then_inc(s["d_hi"], 1)
                    if not last:
                        split_gate_up(n, i + 1)

                with act.Fori(0, FF_PAIRS - 1) as i:
                    turn(i, last=False)
                turn(FF_PAIRS - 1, last=True)

            act.wait_ge(eps_set, 1)
            norm(0, ALL_CHUNKS, take_high, lambda: split_gate_up(0, 0))
            ffn(0, ALL_CHUNKS)

            def split_weights(unit, kind):
                dst = (wq, w_kv, w_kv, wo)[kind]
                index = unit[0] + 4 * unit[1]
                src = stage_a[:, unit[0] % 2, :]
                if kind != 3:
                    src = src.rearrange("p (k f) -> p k f", k=KT)
                act.wait_ge(a_loaded[unit[0] % 2], 16 * (unit[0] // 2 + 1) + 32 * unit[1])
                nc.scalar.activation(dst[:, 0], src, ACT.Copy).then_inc(a_hi, 1)

            def head(hd, first, last):
                base = group_base(hd)

                def group_ready(g):
                    act.wait_ge(grouped, base + g + 1)

                act.wait_ge(grouped, base)
                split_weights((2, 0) if first else (6, hd - 1), 1)
                group_ready(G_Q1)
                nc.scalar.activation(q[:, 0, BANK:], psum[:, Q1_BANK, :], ACT.Copy, scale=Q_SCALE)\
                    .then_inc(proj_hi, 1)
                for c, (t0, t1) in enumerate(VT_GROUPS):
                    rows = META if t0 == META_TILE else P
                    group_ready(G_VT + c)
                    src = psum[0:rows, VT_BANKS[c], 0:(t1 - t0) * P].rearrange("p (t d) -> p t d", d=P)
                    nc.scalar.activation(v[0:rows, 0, t0:t1, :], src, ACT.Copy).then_inc(proj_hi, 1)
                for n, c in enumerate(K_ORDER):
                    at, cols = ALL_CHUNKS[c]
                    group_ready(G_K + n)
                    nc.scalar.activation(k[:, 0, at:at + cols], psum[:, K_BANKS[n], 0:cols], ACT.Copy)\
                        .then_inc(proj_hi, 1)
                for s in range(SLOTS):
                    if s < S:
                        _, tile, _, n, _ = STEPS[s]
                        rows = META if tile == META_TILE else P
                        z, z_sb, e = psum[0:rows, s % 2, 0:n], zs[0:rows, s % 4, 0:n], sp[0:rows, s % 3, 0:n]
                        act.wait_ge(scored, S * hd + s + 1)
                        wait(act, w_done, S * hd + (s - 3 if s >= 4 else 0))
                        nc.scalar.activation(z_sb, z, ACT.Copy).then_inc(z_read, 1)
                        wait(act, sp_lo_done, S * hd + (s - 2 if s >= 3 else 0))
                        nc.scalar.activation(e, z, ACT.Abs).then_inc(z_read, 1)
                        act.wait_ge(z_read, 2 * (S * hd + s + 1))
                        nc.scalar.activation(e, e, ACT.Exp, scale=-1.0).then_inc(exped, 1)
                        act.wait_ge(exped, S * hd + s + 1)
                        nc.scalar.activation(e, e, ACT.Ln, bias=1.0).then_inc(logged, 1)
                    if 2 <= s < S + 2:
                        t = s - 2
                        n, rows = STEPS[t][3], META if STEPS[t][1] == META_TILE else P
                        act.wait_ge(logw_done, S * hd + t + 1)
                        wait(act, w_lo_done, S * hd + (t - 1 if t >= 2 else 0))
                        nc.scalar.activation(wf[0:rows, t % 2, 0:n], zs[0:rows, t % 4, 0:n], ACT.Exp)\
                            .then_inc(w_done, 1)
                    if s == KT - 1:
                        act.wait_ge(q0_grouped, hd + 1)
                        nc.scalar.activation(q[:, 0, 0:BANK], psum[:, Q0_BANK, :], ACT.Copy, scale=Q_SCALE)\
                            .then_inc(proj_hi, 1)
                    if s == 5 and not last:
                        split_weights((3, hd), 2)
                    if s == 9 and not last:
                        split_weights((4, hd), 0)
                    for chunk, slot in ((1, LAST_OF_CHUNK[1] + 5), (0, SLOTS - 1)):
                        if s == slot:
                            act.wait_ge(weighed, S * hd + LAST_OF_CHUNK[chunk] + 1)
                            nc.scalar.activation(o[:, 0, chunk * BANK:(chunk + 1) * BANK], psum[:, 4 + chunk, :],
                                                 ACT.Copy).then_inc(o_hi_done, 1)
                if not first:
                    group_ready(G_O + O_GROUPS - 1)
                split_weights((3, hd) if last else (5, hd), 3)

            def split_first_weights():
                split_weights((0, 0), 2)
                split_weights((1, 0), 0)

            def h_ready(c):
                act.wait_ge(ffns[0]["added"], KT * (len(ALL_CHUNKS) * (FF_PAIRS - 1) + c + 1))

            norm(1, ALL_CHUNKS, h_ready, split_first_weights)
            nc.scalar.preload_act_table_set("natural_log_exp_and_others")
            head(0, first=True, last=False)
            with act.Fori(1, HEADS - 1) as hd:
                head(hd, first=False, last=False)
            head(HEADS - 1, first=False, last=True)

            def h_ready_2(c):
                act.wait_ge(evacuated, GROUPS_BEFORE_LAST_O + KT * (c + 1))

            norm(2, FRAME_CHUNKS, h_ready_2, lambda: split_gate_up(1, 0))
            ffn(1, FRAME_CHUNKS)
            ffn_over(act, 1)

            for t in range(FRAMES // P):
                for half in range(2):
                    m = 2 * t + half
                    act.wait_ge(out_transposed, m + 1)
                    wait(act, out_squared, m - 1)
                    nc.scalar.activation(square_out[:, m % 2, :], psum[:, m % 8, :], ACT.Square,
                                         accum_out=stats[:, t, half:half + 1]).then_inc(out_squared, 1)
                act.wait_ge(out_total, t + 1)
                nc.scalar.activation(stats[:, t, 3:4], stats[:, t, 2:3], ACT.Sqrt, scale=1.0 / D_MODEL,
                                     bias=eps[:, 0:1]).then_inc(out_root, 1)

        @block.vector
        def _(dve):
            nc.vector.memset(eps[:], EPS).then_inc(eps_set, 1)
            for t in range(META_TILE + 1):
                cols = META if t == META_TILE else P
                dve.wait_ge(x_transposed, t + 1)
                src = psum[:, 6 * (t % 2), :].rearrange("p (k c) -> p k c", k=4)[:, :, 0:cols]
                nc.vector.tensor_copy(h[:, 0:4, t * P:t * P + cols], src).then_inc(h_low, 1)

            def norm(n, chunks):
                s = norms[n]

                def lo(c, kt):
                    m, (at, cols) = c * KT + kt, chunks[c]
                    dve.wait_ge(s["hi"], m + 1)
                    nc.vector.tensor_tensor(u_lo[:, kt, at:at + cols], un[:, m % 3, 0:cols],
                                            u_hi[:, kt, at:at + cols].bitcast(F32), ALU.subtract)\
                        .then_inc(s["lo"], 1)

                for c, (at, cols) in enumerate(chunks):
                    dve.wait_ge(s["root"], c + 1)
                    nc.vector.reciprocal(rstd[:, c % 2, 0:cols], rstd[:, c % 2, 0:cols]).then_inc(s["rstd"], 1)
                    dve.wait_ge(s["rstd"], c + 1)
                    for kt in range(KT):
                        m = c * KT + kt
                        wait(dve, s["lo"], m - 2)
                        nc.vector.scalar_tensor_tensor(out=un[:, m % 3, 0:cols], in0=h[:, kt, at:at + cols],
                                                       scalar=gains[:, n, kt:kt + 1], in1=rstd[:, c % 2, 0:cols],
                                                       op0=ALU.mult, op1=ALU.mult).then_inc(s["un"], 1)
                        if kt:
                            lo(c, kt - 1)
                    lo(c, KT - 1)
                norm_over(dve, n)

            def ffn(n, chunks):
                s = ffns[n]
                per_turn, adds = 2 * len(chunks), KT * len(chunks)
                with dve.Fori(0, FF_PAIRS) as i:
                    for c, (at, cols) in enumerate(chunks):
                        for ft in range(2):
                            m = 2 * c + ft
                            dve.wait_ge(s["silu"], per_turn * i + m + 1)
                            dve.wait_ge(s["up"], per_turn * i + m + 1)
                            if m >= 2:
                                dve.wait_ge(s["hid_lo"], per_turn * i + m - 1)
                            nc.vector.tensor_tensor(hidden[:, m % 2, 0:cols], silu_g[:, m % 2, 0:cols],
                                                    psum[:, 2 * (m % 2) + 1, 0:cols], ALU.mult)\
                                .then_inc(s["hidden"], 1)
                            dve.wait_ge(s["hid_hi"], per_turn * i + m + 1)
                            nc.vector.tensor_tensor(hid_lo[:, ft, at:at + cols], hidden[:, m % 2, 0:cols],
                                                    hid_hi[:, ft, at:at + cols].bitcast(F32), ALU.subtract)\
                                .then_inc(s["hid_lo"], 1)
                    for c, (at, cols) in enumerate(chunks):
                        for dt in range(KT):
                            m = c * KT + dt
                            dve.wait_ge(s["down"], adds * i + m + 1)
                            nc.vector.scalar_tensor_tensor(out=h[:, dt, at:at + cols], in0=psum[:, 4 + m % 4, 0:cols],
                                                           scalar=0.5, in1=h[:, dt, at:at + cols],
                                                           op0=ALU.mult, op1=ALU.add).then_inc(s["added"], 1)

            def take_v(c, groups_before):
                at, cols = ALL_CHUNKS[c]
                dve.wait_ge(grouped, groups_before + c + 1)
                nc.vector.tensor_copy(v_t[:, at:at + cols], psum[:, V_BANKS[c], 0:cols]).then_inc(evacuated, 1)

            def head(hd, first, last):
                base = group_base(hd)

                def group_ready(g):
                    dve.wait_ge(grouped, base + g + 1)

                def lo(dst, src, hi, scale=None, freed=evacuated):
                    if scale is None:
                        done = nc.vector.tensor_tensor(dst, src, hi.bitcast(F32), ALU.subtract)
                    else:
                        done = nc.vector.scalar_tensor_tensor(out=dst, in0=src, scalar=scale, in1=hi.bitcast(F32),
                                                              op0=ALU.mult, op1=ALU.subtract)
                    done.then_inc(freed, 1)

                dve.wait_ge(proj_hi, 8 * hd + 1)
                lo(q[:, 1, BANK:], psum[:, Q1_BANK, :], q[:, 0, BANK:], Q_SCALE)
                for c, (t0, t1) in enumerate(VT_GROUPS):
                    rows = META if t0 == META_TILE else P
                    dve.wait_ge(proj_hi, 8 * hd + 2 + c)
                    src = psum[0:rows, VT_BANKS[c], 0:(t1 - t0) * P].rearrange("p (t d) -> p t d", d=P)
                    lo(v[0:rows, 1, t0:t1, :], src, v[0:rows, 0, t0:t1, :])
                for n, c in enumerate(K_ORDER):
                    at, cols = ALL_CHUNKS[c]
                    dve.wait_ge(proj_hi, 8 * hd + 5 + n)
                    lo(k[:, 1, at:at + cols], psum[:, K_BANKS[n], 0:cols], k[:, 0, at:at + cols])
                for s in range(SLOTS):
                    if 2 <= s < S + 2:
                        t = s - 2
                        chunk, tile, at, n, _ = STEPS[t]
                        rows = META if tile == META_TILE else P
                        at -= chunk * BANK
                        dve.wait_ge(summed, S * hd + t + 1)
                        nc.vector.tensor_tensor(zs[0:rows, t % 4, 0:n], zs[0:rows, t % 4, 0:n],
                                                psum[0:rows, 2 + chunk, at:at + n], ALU.subtract)\
                            .then_inc(logw_done, 1)
                    if s < S:
                        n, rows = STEPS[s][3], META if STEPS[s][1] == META_TILE else P
                        e = sp[0:rows, s % 3, 0:n]
                        dve.wait_ge(logged, S * hd + s + 1)
                        nc.vector.scalar_tensor_tensor(out=e, in0=zs[0:rows, s % 4, 0:n], scalar=0.0, in1=e,
                                                       op0=ALU.max, op1=ALU.add).then_inc(softplused, 1)
                    if s < O_GROUPS and not first:
                        group_ready(G_O + s)
                        add_output(s, O_BANK)
                    if s < S:
                        dve.wait_ge(softplused, S * hd + s + 1)
                        if s >= 2 and STEPS[s - 2][1] == META_TILE:
                            dve.wait_ge(summed, S * hd + s - 1)
                        elif s >= 2:
                            dve.wait_ge(completed, COMPLETIONS * hd + completions_before(s - 1))
                        nc.vector.tensor_copy(sp_hi[0:rows, s % 2, 0:n], e).then_inc(sp_hi_done, 1)
                    if 2 <= s < S + 2:
                        t = s - 2
                        n, rows = STEPS[t][3], META if STEPS[t][1] == META_TILE else P
                        dve.wait_ge(w_done, S * hd + t + 1)
                        wait(dve, weighed, S * hd + (t - 1 if t >= 2 else 0))
                        nc.vector.tensor_copy(w_hi[0:rows, t % 2, 0:n], wf[0:rows, t % 2, 0:n])\
                            .then_inc(w_hi_done, 1)
                    if s == KT - 1:
                        dve.wait_ge(proj_hi, 8 * hd + 8)
                        lo(q[:, 1, 0:BANK], psum[:, Q0_BANK, :], q[:, 0, 0:BANK], Q_SCALE, q0_evacuated)
                    if s == SLOTS - 1 and not last:
                        take_v(0, base + first_v_group(first))
                        take_v(1, base + first_v_group(first))
                    for chunk, slot in ((1, LAST_OF_CHUNK[1] + 5), (0, SLOTS - 1)):
                        if s == slot:
                            cols = slice(chunk * BANK, (chunk + 1) * BANK)
                            dve.wait_ge(o_hi_done, 2 * hd + 2 - chunk)
                            nc.vector.tensor_tensor(o[:, 1, cols], psum[:, 4 + chunk, :], o[:, 0, cols].bitcast(F32),
                                                    ALU.subtract).then_inc(o_lo_done, 1)
                if not last:
                    take_v(2, base + first_v_group(first))

            def add_output(g, bank):
                dt, chunk = g % KT, 1 - g // KT
                cols = slice(chunk * BANK, (chunk + 1) * BANK)
                nc.vector.tensor_tensor(h[:, dt, cols], psum[:, bank, :], h[:, dt, cols], ALU.add)\
                    .then_inc(evacuated, 1)

            dve.wait_ge(gains_loaded, 16)
            dve.wait_ge(h_low, META_TILE + 1)
            dve.wait_ge(h_high, META_TILE + 1)
            norm(0, ALL_CHUNKS)
            ffn(0, ALL_CHUNKS)
            ffn_over(dve, 0)
            norm(1, ALL_CHUNKS)
            for c in range(V_GROUPS):
                take_v(c, 0)
            head(0, first=True, last=False)
            with dve.Fori(1, HEADS - 1) as hd:
                head(hd, first=False, last=False)
            head(HEADS - 1, first=False, last=True)
            for n, g in enumerate(LAST_O_ORDER):
                dve.wait_ge(grouped, GROUPS_BEFORE_LAST_O + n + 1)
                add_output(g, 6 + g % 2)
            attention_over(dve)
            norm(2, FRAME_CHUNKS)
            ffn(1, FRAME_CHUNKS)

            dve.wait_ge(gain_loaded, 16)

            def scale_rows(t):
                if t >= 4:
                    dve.wait_ge(out_stored[t % 4], 16 * (t // 4))
                dve.wait_ge(out_rstd, t + 1)
                for half in range(2):
                    cols = slice(half * BANK, (half + 1) * BANK)
                    nc.vector.scalar_tensor_tensor(out=out_tiles[:, t % 4, cols], in0=psum[:, (2 * t + half) % 8, :],
                                                   scalar=stats[:, t, 3:4], in1=gain_row[:, cols],
                                                   op0=ALU.mult, op1=ALU.mult).then_inc(out_scaled, 1)

            for t in range(FRAMES // P):
                dve.wait_ge(out_squared, 2 * t + 2)
                nc.vector.tensor_tensor(stats[:, t, 2:3], stats[:, t, 0:1], stats[:, t, 1:2], ALU.add)\
                    .then_inc(out_total, 1)
                if t:
                    scale_rows(t - 1)
                dve.wait_ge(out_root, t + 1)
                nc.vector.reciprocal(stats[:, t, 3:4], stats[:, t, 3:4]).then_inc(out_rstd, 1)
            scale_rows(FRAMES // P - 1)

        @block.tensor
        def _(pe):
            def product(dst, w_halves, x_halves, start, stop):
                (wh, wl), (xh, xl) = w_halves, x_halves
                nc.tensor.matmul(dst, wh, xh, start=start, stop=False, skip_group_check=True)
                nc.tensor.matmul(dst, wh, xl, start=False, stop=False, skip_group_check=True)
                return nc.tensor.matmul(dst, wl, xh, start=False, stop=stop, skip_group_check=True)

            def transpose_x(c):
                for t in X_TILES[c]:
                    rows = META if t == META_TILE else P
                    pe.wait_ge(x_loaded[t % 4], 16 * (t // 4 + 1))
                    if t >= 2:
                        pe.wait_ge(h_low, t - 1)
                        pe.wait_ge(h_high, t - 1)
                    for kt in range(KT):
                        dst = psum[:, 6 * (t % 2) + kt // 4, (kt % 4) * P:(kt % 4) * P + rows]
                        last = nc.tensor.transpose(dst, x_tiles[0:rows, t % 4, kt * P:(kt + 1) * P],
                                                   ident[0:rows, 0:rows])
                    last.then_inc(x_transposed, 1)

            def sums(n, c):
                s = norms[n]
                cols = (FRAME_CHUNKS if n == 2 else ALL_CHUNKS)[c][1]
                for kt in range(KT):
                    m = c * KT + kt
                    pe.wait_ge(s["squared"], m + 1)
                    nc.tensor.matmul(psum[:, NORM_BANKS[n] + c, 0:cols], ones[:], sq[:, m % 3, 0:cols],
                                     start=kt == 0, stop=kt == KT - 1).then_inc(s["summed"], 1)

            def ffn(n, chunks):
                s = ffns[n]
                per_turn, adds = 2 * len(chunks), KT * len(chunks)

                def gate_up(i):
                    for c, (at, cols) in enumerate(chunks):
                        pe.wait_ge(norms[n * 2]["lo"], KT * (c + 1))
                        for ft in range(2):
                            m = 2 * c + ft
                            if m >= 2:
                                pe.wait_ge(s["hidden"], per_turn * i + m - 1)
                            for w, split, done, bank in ((wg, "g_split", "gate", 0), (wu, "u_split", "up", 1)):
                                if m == 0:
                                    pe.wait_ge(s[split], i + 1)
                                f = slice(ft * P, (ft + 1) * P)
                                for kt in range(KT):
                                    last = product(psum[:, 2 * (m % 2) + bank, 0:cols],
                                                   (w[:, 0, kt, f], w[:, 1, kt, f]),
                                                   (u_hi[:, kt, at:at + cols], u_lo[:, kt, at:at + cols]),
                                                   start=kt == 0, stop=kt == KT - 1)
                                last.then_inc(s[done], 1)
                    pe.wait_ge(s["d_split"], i + 1)

                def down(i, c):
                    at, cols = chunks[c]
                    pe.wait_ge(s["hid_lo"], per_turn * i + 2 * c + 2)
                    for dt in range(KT):
                        m = c * KT + dt
                        if m >= 4:
                            pe.wait_ge(s["added"], adds * i + m - 3)
                        d = slice(dt * P, (dt + 1) * P)
                        for ft in range(2):
                            last = product(psum[:, 4 + m % 4, 0:cols], (wd[:, 0, ft, d], wd[:, 1, ft, d]),
                                           (hid_hi[:, ft, at:at + cols], hid_lo[:, ft, at:at + cols]),
                                           start=ft == 0, stop=ft == 1)
                        last.then_inc(s["down"], 1)

                with pe.Fori(0, FF_PAIRS - 1) as i:
                    gate_up(i)
                    for c in range(len(chunks)):
                        down(i, c)
                gate_up(FF_PAIRS - 1)
                down(FF_PAIRS - 1, 0)
                down(FF_PAIRS - 1, 1)
                if n == 0:
                    sums(1, 0)
                    sums(1, 1)
                    down(FF_PAIRS - 1, 2)

            def output_group(g, bank):
                dt, chunk = g % KT, 1 - g // KT
                cols, d = slice(chunk * BANK, (chunk + 1) * BANK), slice(dt * P, (dt + 1) * P)
                product(psum[:, bank, :], (wo[:, 0, d], wo[:, 1, d]),
                        (o[:, 0, cols], o[:, 1, cols]), start=True, stop=True).then_inc(grouped, 1)

            def project(bank, w, at, cols, kts, done):
                for kt in kts:
                    last = product(psum[:, bank, 0:cols], (w[:, 0, kt, :], w[:, 1, kt, :]),
                                   (u_hi[:, kt, at:at + cols], u_lo[:, kt, at:at + cols]),
                                   start=kt == 0, stop=kt == KT - 1)
                if kts[-1] == KT - 1:
                    last.then_inc(done, 1)

            def project_v(c):
                project(V_BANKS[c], w_kv, *ALL_CHUNKS[c], range(KT), grouped)

            def head(hd, first, last):
                base = group_base(hd)

                def bank_free(g):
                    pe.wait_ge(evacuated, base + g - 1)

                units = 4 * hd
                bank_free(G_Q1)
                pe.wait_ge(a_split, 2 if first else units + 1)
                project(Q1_BANK, wq, BANK, BANK, range(KT), grouped)
                pe.wait_ge(evacuated, base)
                for c, (t0, t1) in enumerate(VT_GROUPS):
                    for t in range(t0, t1):
                        rows = META if t == META_TILE else P
                        dst = psum[0:rows, VT_BANKS[c], (t - t0) * P:(t - t0 + 1) * P]
                        done = nc.tensor.transpose(dst, v_t[:, t * P:t * P + rows], ident[:])
                    done.then_inc(grouped, 1)
                pe.wait_ge(a_split, units + 3)
                for n, c in enumerate(K_ORDER):
                    if n == 1:
                        pe.wait_ge(evacuated, base + 1)
                    project(K_BANKS[n], w_kv, *ALL_CHUNKS[c], range(KT), grouped)

                def score(t):
                    _, tile, at, n, mask_at = STEPS[t]
                    rows = META if tile == META_TILE else P
                    keys = slice(tile * P, tile * P + rows)
                    if t < 2:
                        pe.wait_ge(evacuated, base + G_O - 1 + t)
                    if t == LAST_OF_CHUNK[1] + 1:
                        pe.wait_ge(q0_evacuated, hd + 1)
                    if t >= 2:
                        pe.wait_ge(z_read, 2 * (S * hd + t - 1))
                    dst = psum[0:rows, t % 2, 0:n]
                    last = product(dst, (k[:, 0, keys], k[:, 1, keys]), (q[:, 0, at:at + n], q[:, 1, at:at + n]),
                                   start=True, stop=mask_at is None)
                    if mask_at is not None:
                        last = nc.tensor.matmul(psum[:, t % 2, 0:2 * P], ident_r[:], mask[:, mask_at:mask_at + 2 * P],
                                                start=False, stop=True, skip_group_check=True)
                    last.then_inc(scored, 1)

                def running_sum(t, triangle, start, stop):
                    chunk, tile, at, n, _ = STEPS[t]
                    rows = META if tile == META_TILE else P
                    at -= chunk * BANK
                    dst = psum[:, 2 + chunk, at:at + n]
                    nc.tensor.matmul(dst, triangle[0:rows, :], sp_hi[0:rows, t % 2, 0:n],
                                     start=start, stop=False, skip_group_check=True)
                    return nc.tensor.matmul(dst, triangle[0:rows, :], sp_lo[0:rows, t % 2, 0:n],
                                            start=False, stop=stop, skip_group_check=True)

                def weigh(t):
                    chunk, tile, at, n, _ = STEPS[t]
                    rows = META if tile == META_TILE else P
                    at -= chunk * BANK
                    start = t == 0 or STEPS[t - 1][0] != chunk
                    if t == 0:
                        pe.wait_ge(evacuated, base + G_O)
                    if start:
                        wait(pe, o_lo_done, 2 * hd - chunk)
                    pe.wait_ge(w_lo_done, S * hd + t + 1)
                    product(psum[:, 4 + chunk, at:at + n], (v[0:rows, 0, tile, :], v[0:rows, 1, tile, :]),
                            (w_hi[0:rows, t % 2, 0:n], w_lo[0:rows, t % 2, 0:n]),
                            start=start, stop=tile == META_TILE).then_inc(weighed, 1)

                for s in range(SLOTS):
                    if s < S:
                        score(s)
                    if s < KT:
                        project(Q0_BANK, wq, 0, BANK, range(s, s + 1), q0_grouped)
                    t = s - 2
                    if 0 <= t < S:
                        start = t == 0 or STEPS[t - 1][0] != STEPS[t][0]
                        pe.wait_ge(sp_lo_done, S * hd + t + 1)
                        running_sum(t, tri, start, STEPS[t][1] == META_TILE).then_inc(summed, 1)
                    if V_FIRST_SLOT <= s < V_SLOT and not last:
                        kt = s - V_FIRST_SLOT
                        if kt == 0:
                            pe.wait_ge(a_split, units + 4)
                            pe.wait_ge(q0_evacuated, hd + 1)
                        project(V_BANKS[0], w_kv, *ALL_CHUNKS[0], range(kt, kt + 1), grouped)
                    if 0 <= s - 4 < S:
                        weigh(s - 4)
                    if s < O_GROUPS and not first:
                        if s == 0:
                            pe.wait_ge(a_split, units + 2)
                            pe.wait_ge(o_lo_done, 2 * hd)
                        if s:
                            pe.wait_ge(evacuated, base + G_O + s)
                        output_group(s, O_BANK)
                    if 0 <= t < S and STEPS[t][1] != META_TILE:
                        pe.wait_ge(logw_done, S * hd + t + 1)
                        running_sum(t, tri_rest, False, False).then_inc(completed, 1)
                    if V_SLOT <= s + 1 < V_SLOT + V_GROUPS - 1 and not last:
                        c = s + 2 - V_SLOT
                        bank_free(first_v_group(first) + c)
                        project_v(c)

            pe.wait_ge(const_set, CONSTANTS)
            for c in range(len(ALL_CHUNKS)):
                transpose_x(c)
                sums(0, c)
            ffn(0, ALL_CHUNKS)
            sums(1, 2)
            pe.wait_ge(a_split, 1)
            for c in range(V_GROUPS):
                pe.wait_ge(norms[1]["lo"], KT * (c + 1))
                wait(pe, evacuated, c - 1)
                project_v(c)
            head(0, first=True, last=False)
            with pe.Fori(1, HEADS - 1) as hd:
                head(hd, first=False, last=False)
            head(HEADS - 1, first=False, last=True)
            pe.wait_ge(a_split, 4 * HEADS)
            pe.wait_ge(o_lo_done, 2 * HEADS)
            for n, g in enumerate(LAST_O_ORDER):
                pe.wait_ge(evacuated, GROUPS_BEFORE_LAST_O + (n - 1 if n else 0))
                output_group(g, 6 + g % 2)
            sums(2, 0)
            sums(2, 1)
            ffn(1, FRAME_CHUNKS)

            ffn_over(pe, 1)
            for t in range(FRAMES // P):
                if t >= 4:
                    pe.wait_ge(out_scaled, 2 * (t - 3))
                for kt in range(KT):
                    last = nc.tensor.transpose(psum[:, (2 * t + kt // 4) % 8, (kt % 4) * P:(kt % 4 + 1) * P],
                                               h[:, kt, t * P:(t + 1) * P], ident[:])
                    if kt % 4 == 3:
                        last.then_inc(out_transposed, 1)


def kernel(**inputs):
    import numpy as np
    import concourse.bacc as bacc
    from concourse.bass_utils import run_bass_kernel_spmd

    nc = bacc.Bacc("TRN2", target_bir_lowering=False, num_devices=1)
    gains = np.stack([np.asarray(inputs[name][0]).reshape(KT, P).T for name in ("ffn1_norm", "mix_norm", "ffn2_norm")],
                     axis=1)
    arrays = {
        "x": inputs["x"][0], "meta": inputs["meta_tokens"],
        "gains": gains, "w1_in": inputs["ffn1_w_in"][0], "w1_out": inputs["ffn1_w_out"][0],
        "w2_in": inputs["ffn2_w_in"][0], "w2_out": inputs["ffn2_w_out"][0],
        "w_qkv": inputs["sb_w_qkv"][0], "w_o": inputs["sb_w_o"][0], "g_final": inputs["final_norm"],
    }
    arrays = {name + "_dram": np.ascontiguousarray(a) for name, a in arrays.items()}
    args = [nc.dram_tensor(name, a.shape, mybir.dt.from_np(a.dtype), kind="ExternalInput").ap()
            for name, a in arrays.items()]
    out = nc.dram_tensor("out_dram", (FRAMES, D_MODEL), F32, kind="ExternalOutput").ap()
    build(nc, *args, out)
    r = run_bass_kernel_spmd(nc, [arrays], core_ids=[0])
    return r.results[0]["out_dram"].reshape(1, FRAMES, D_MODEL)
```

```python
from contextlib import ExitStack

import concourse.bass as bass
from concourse import mybir

F32 = mybir.dt.float32
F32R = mybir.dt.float32r
ALU = mybir.AluOpType
ACT = mybir.ActivationFunctionType

P = 128
BANK = 512
FRAMES, META, D_MODEL = 1024, 16, 1024
TOKENS = FRAMES + META
KT = D_MODEL // P
D_FF = 2816
FF_PAIRS = D_FF // (2 * P)
HEADS = 8
EPS = 1e-5
Q_SCALE = float(P) ** -0.5
NEG = -1e30

ALL_CHUNKS = [(0, 348), (348, 348), (696, 344)]
FRAME_CHUNKS = [(0, BANK), (BANK, BANK)]

META_TILE = FRAMES // P

X_TILES = [range(0, 3), range(3, 6), range(6, META_TILE + 1)]


def attention_steps():
    steps = []
    for chunk in (1, 0):
        q_begin, q_end = chunk * BANK, (chunk + 1) * BANK
        for tile in range(q_end // P - 1, -1, -1):
            first = min(max(tile * P, q_begin), q_end - 2 * P)
            mask = None if tile * P < q_begin else P - (tile * P - first)
            steps.append((chunk, tile, first, q_end - first, mask))
        steps.append((chunk, META_TILE, q_begin, BANK, None))
    return steps


STEPS = attention_steps()
S = len(STEPS)
COMPLETIONS = sum(tile != META_TILE for _, tile, _, _, _ in STEPS)
LAST_OF_CHUNK = {chunk: max(t for t in range(S) if STEPS[t][0] == chunk) for chunk in (0, 1)}
SLOTS = S + 4

G_Q1, G_VT, G_K, G_O = 0, 1, 4, 7
K_ORDER = (2, 1, 0)
O_GROUPS, V_GROUPS = 16, 3
LAST_O_ORDER = [*range(KT, 2 * KT), *range(KT)]
LAST_O_BANKS = (6, 7, 0, 1)
LAST_O_SPLITS = (LAST_OF_CHUNK[1] + 2, S + 1)
LAST_O_AHEAD = 3
Q1_BANK, VT_BANKS, K_BANKS, V_BANKS = 7, (0, 1, 2), (6, 7, 3), (6, 7, 6)
FIRST_V_BANKS = (6, 7, 5)
Q0_BANK, O_BANK = 6, 7
VT_GROUPS = [(0, 4), (4, 8), (8, 9)]
V_FIRST_SLOT = KT + 1
V_SLOT = V_FIRST_SLOT + KT
OLD_GROUPS = V_GROUPS + G_O + V_GROUPS
GROUPS = G_O + O_GROUPS + V_GROUPS


def first_v_group(first):
    return G_O if first else G_O + O_GROUPS


def group_base(h):
    return V_GROUPS if isinstance(h, int) and h == 0 else GROUPS * h - (GROUPS - OLD_GROUPS)


GROUPS_BEFORE_LAST_O = GROUPS * HEADS - (GROUPS - OLD_GROUPS) - V_GROUPS


def completions_before(t):
    return sum(STEPS[s][1] != META_TILE for s in range(t))


def pool_splits(n, c, kt):
    return kt % 2 == 1 and not (n == 0 and (c == 1 or c == 0 and kt > 3))


def wait(engine, semaphore, value):
    if isinstance(value, int) and value <= 0:
        return
    engine.wait_ge(semaphore, value)


def build(nc, x, meta, gains_in, w1_in, w1_out, w2_in, w2_out, w_qkv, w_o, g_final, out):
    ctx = ExitStack()
    with ctx:
        def sbuf(name, shape, dtype):
            return ctx.enter_context(nc.sbuf_tensor(name, shape, dtype))

        def sem(name):
            return ctx.enter_context(nc.semaphore(name))

        h = sbuf("h", [P, KT, TOKENS], F32)
        u_hi = sbuf("u_hi", [P, KT, TOKENS], F32R)
        u_lo = sbuf("u_lo", [P, KT, TOKENS], F32R)
        scratch = sbuf("scratch", [P, 8192], F32)
        work = sbuf("work", [P, 18720], F32R)
        tri = sbuf("tri", [P, P], F32R)
        tri_rest = sbuf("tri_rest", [P, P], F32R)
        ident_r = sbuf("ident_r", [P, P], F32R)
        mask = sbuf("mask", [P, 3 * P], F32R)
        ident = sbuf("ident", [P, P], F32)
        ones = sbuf("ones", [P, P], F32)
        gains = sbuf("gains", [P, 3, KT], F32)
        stats = sbuf("stats", [P, KT, 4], F32)
        eps = sbuf("eps", [P, 1], F32)
        psum = ctx.enter_context(nc.psum_tensor("psum", [P, 8, BANK], F32))

        def piece(arena, at, *dims):
            size = 1
            for n in dims:
                size *= n
            flat = arena[:, at:at + size]
            if len(dims) == 2:
                return flat.rearrange("p (a b) -> p a b", a=dims[0])
            if len(dims) == 3:
                return flat.rearrange("p (a b c) -> p a b c", a=dims[0], b=dims[1])
            return flat

        x_tiles = piece(scratch, 0, 4, D_MODEL)
        sq = piece(scratch, 4096, 3, BANK)
        rstd = piece(scratch, 5632, 2, BANK)
        un = piece(scratch, 6656, 3, BANK)
        stage_g = piece(scratch, 0, KT, 2 * P)
        stage_u = piece(scratch, 2048, KT, 2 * P)
        stage_d = piece(scratch, 4096, 2, D_MODEL)
        silu_g = piece(scratch, 6144, 2, BANK)
        hidden = piece(scratch, 7168, 2, BANK)
        stage_a = piece(scratch, 0, 2, D_MODEL)
        zs = piece(scratch, 2048, 4, BANK)
        sp = piece(scratch, 4096, 3, BANK)
        wf = piece(scratch, 5632, 2, BANK)
        v_t = piece(scratch, 6656, TOKENS)
        out_tiles = piece(scratch, 0, 4, D_MODEL)
        gain_row = piece(scratch, 4096, D_MODEL)
        square_out = piece(scratch, 6144, 2, BANK)

        wg = piece(work, 0, 2, KT, 2 * P)
        wu = piece(work, 4096, 2, KT, 2 * P)
        wd = piece(work, 8192, 2, 2, D_MODEL)
        hid_hi = piece(work, 12288, 2, TOKENS)
        hid_lo = piece(work, 14368, 2, TOKENS)
        wq = piece(work, 0, 2, KT, P)
        w_kv = piece(work, 2048, 2, KT, P)
        wo = piece(work, 4096, 2, D_MODEL)
        q = piece(work, 6144, 2, FRAMES)
        k = piece(work, 8192, 2, TOKENS)
        wo_last = (k[:, :, BANK:2 * BANK], k[:, :, 0:BANK])
        v = piece(work, 10272, 2, META_TILE + 1, P)
        o = piece(work, 12576, 2, FRAMES)
        sp_hi = piece(work, 14624, 2, BANK)
        sp_lo = piece(work, 15648, 2, BANK)
        w_hi = piece(work, 16672, 2, BANK)
        w_lo = piece(work, 17696, 2, BANK)

        const_set = sem("const_set")
        gains_loaded = sem("gains_loaded")
        x_loaded = [sem(f"x_loaded{i}") for i in range(4)]
        x_transposed = sem("x_transposed")
        h_low = sem("h_low")
        h_high = sem("h_high")
        norms = [{name: sem(f"norm{n}_{name}") for name in
                  ("squared", "summed", "root", "rstd", "un", "hi", "lo", "lo_pool")} for n in range(3)]
        ffns = [{name: sem(f"ffn{n}_{name}") for name in
                 ("g_loaded", "u_loaded", "d_loaded", "g_hi", "u_hi", "d_hi", "g_split", "u_split",
                  "d_split", "gate", "up", "silu", "hidden", "hid_hi", "hid_lo", "down", "added")}
                for n in range(2)]
        a_loaded = [sem(f"a_loaded{i}") for i in range(2)]
        a_hi = sem("a_hi")
        a_split = sem("a_split")
        grouped = sem("grouped")
        evacuated = sem("evacuated")
        q0_grouped = sem("q0_grouped")
        q0_evacuated = sem("q0_evacuated")
        proj_hi = sem("proj_hi")
        scored = sem("scored")
        z_read = sem("z_read")
        eps_set = sem("eps_set")
        exped = sem("exped")
        logged = sem("logged")
        softplused = sem("softplused")
        sp_hi_done = sem("sp_hi_done")
        sp_lo_done = sem("sp_lo_done")
        summed = sem("summed")
        completed = sem("completed")
        logw_done = sem("logw_done")
        w_done = sem("w_done")
        w_hi_done = sem("w_hi_done")
        w_lo_done = sem("w_lo_done")
        weighed = sem("weighed")
        o_hi_done = sem("o_hi_done")
        o_lo_done = sem("o_lo_done")
        gain_loaded = sem("gain_loaded")
        out_transposed = sem("out_transposed")
        out_squared = sem("out_squared")
        out_total = sem("out_total")
        out_root = sem("out_root")
        out_rstd = sem("out_rstd")
        out_scaled = sem("out_scaled")
        out_stored = [sem(f"out_stored{i}") for i in range(4)]

        CONSTANTS = 8
        NORM_BANKS = (3, 0, 3)

        def ffn_over(engine, n):
            chunks = len(ALL_CHUNKS) if n == 0 else len(FRAME_CHUNKS)
            engine.wait_ge(ffns[n]["added"], FF_PAIRS * chunks * KT)

        def split_through(engine, n, m):
            by_pool = sum(pool_splits(n, i // KT, i % KT) for i in range(m + 1))
            wait(engine, norms[n]["lo"], m + 1 - by_pool)
            wait(engine, norms[n]["lo_pool"], by_pool)

        def norm_over(engine, n):
            split_through(engine, n, KT * (len(FRAME_CHUNKS) if n == 2 else len(ALL_CHUNKS)) - 1)

        block = ctx.enter_context(nc.Block())

        @block.sync
        def _(sp_eng):
            def load_x(t):
                rows = META if t == META_TILE else P
                src = meta[:, :] if t == META_TILE else x[t * P:(t + 1) * P, :]
                if t >= 4:
                    sp_eng.wait_ge(x_transposed, t - 3)
                sp_eng.dma_start(x_tiles[0:rows, t % 4, :], src).then_inc(x_loaded[t % 4], 16)

            def ffn_sources(n, i):
                w_in, w_out = (w1_in, w1_out) if n == 0 else (w2_in, w2_out)
                gate = w_in[:, bass.ds(i * (2 * P), 2 * P)].rearrange("(k p) f -> p k f", p=P)
                up = w_in[:, bass.ds((i + FF_PAIRS) * (2 * P), 2 * P)].rearrange("(k p) f -> p k f", p=P)
                down = w_out[bass.ds(i * (2 * P), 2 * P), :].rearrange("(t p) d -> p t d", p=P)
                return gate, up, down

            def ffn_rest(n):
                s = ffns[n]
                with sp_eng.Fori(1, FF_PAIRS) as i:
                    gate, up, down = ffn_sources(n, i)
                    sp_eng.wait_ge(s["g_split"], i)
                    sp_eng.dma_start(stage_g, gate).then_inc(s["g_loaded"], 16)
                    sp_eng.wait_ge(s["u_split"], i)
                    sp_eng.dma_start(stage_u, up).then_inc(s["u_loaded"], 16)
                    sp_eng.wait_ge(s["d_split"], i)
                    sp_eng.dma_start(stage_d, down).then_inc(s["d_loaded"], 16)

            load_x(0)
            sp_eng.dma_start(gains[:], gains_in[:, :, :]).then_inc(gains_loaded, 16)
            for t in range(1, META_TILE + 1):
                load_x(t)
            gate, up, down = ffn_sources(0, 0)
            sp_eng.wait_ge(x_transposed, META_TILE + 1)
            sp_eng.dma_start(stage_g, gate).then_inc(ffns[0]["g_loaded"], 16)
            sp_eng.dma_start(stage_u, up).then_inc(ffns[0]["u_loaded"], 16)
            norm_over(sp_eng, 0)
            sp_eng.dma_start(stage_d, down).then_inc(ffns[0]["d_loaded"], 16)
            ffn_rest(0)

            def load_a(unit, kind, head):
                slot = unit[0] % 2
                if kind == 3:
                    src = w_o[bass.ds(head * P, P), :]
                else:
                    src = w_qkv[:, bass.ds((head + kind * HEADS) * P, P)].rearrange("(k p) f -> p k f", p=P)
                dst = stage_a[:, slot, :]
                if kind != 3:
                    dst = dst.rearrange("p (k f) -> p k f", k=KT)
                wait(sp_eng, a_split, unit[0] - 1 + 4 * unit[1])
                sp_eng.dma_start(dst, src).then_inc(a_loaded[slot], 16)

            sp_eng.wait_ge(ffns[0]["g_split"], FF_PAIRS)
            load_a((0, 0), 2, 0)
            load_a((1, 0), 0, 0)
            load_a((2, 0), 1, 0)
            with sp_eng.Fori(0, HEADS - 1) as hd:
                load_a((3, hd), 2, hd + 1)
                load_a((4, hd), 0, hd + 1)
                load_a((5, hd), 3, hd)
                load_a((6, hd), 1, hd + 1)
            load_a((3, HEADS - 1), 3, HEADS - 1)

            gate, up, down = ffn_sources(1, 0)
            sp_eng.wait_ge(a_split, 4 * HEADS + 1)
            sp_eng.dma_start(stage_g, gate).then_inc(ffns[1]["g_loaded"], 16)
            sp_eng.wait_ge(w_done, S * HEADS)
            sp_eng.dma_start(stage_u, up).then_inc(ffns[1]["u_loaded"], 16)
            norm_over(sp_eng, 2)
            sp_eng.dma_start(stage_d, down).then_inc(ffns[1]["d_loaded"], 16)
            ffn_rest(1)

            sp_eng.wait_ge(ffns[1]["d_split"], FF_PAIRS)
            sp_eng.dma_start(gain_row, g_final.rearrange("(a n) -> a n", a=1).to_broadcast([P, D_MODEL]))\
                .then_inc(gain_loaded, 16)
            for t in range(FRAMES // P):
                sp_eng.wait_ge(out_scaled, 2 * (t + 1))
                sp_eng.dma_start(out[t * P:(t + 1) * P, :], out_tiles[:, t % 4, :]).then_inc(out_stored[t % 4], 16)
            for slot in range(4):
                sp_eng.wait_ge(out_stored[slot], 16 * (FRAMES // P // 4))

        @block.gpsimd
        def _(pool):
            nc.gpsimd.memset(ident[:], 0.0).then_inc(const_set, 1)
            nc.gpsimd.memset(ones[:], 1.0).then_inc(const_set, 1)
            nc.gpsimd.memset(h[:, 0, 0:3 * P], 0.0).then_inc(const_set, 1)
            pool.wait_ge(const_set, 3)
            nc.gpsimd.affine_select(out=ident[:], in_=ident[:], compare_op=ALU.not_equal, fill=1.0, base=0,
                                    pattern=[[-1, P]], channel_multiplier=1).then_inc(const_set, 1)
            nc.gpsimd.affine_select(out=tri[:], in_=ones[:], compare_op=ALU.is_ge, fill=0.0, base=0,
                                    pattern=[[-1, P]], channel_multiplier=1).then_inc(const_set, 1)
            nc.gpsimd.affine_select(out=tri_rest[:], in_=ones[:], compare_op=ALU.is_gt, fill=0.0, base=0,
                                    pattern=[[1, P]], channel_multiplier=-1).then_inc(const_set, 1)
            nc.gpsimd.affine_select(out=mask[:], in_=h[:, 0, 0:3 * P], compare_op=ALU.is_gt, fill=NEG, base=-P,
                                    pattern=[[1, 3 * P]], channel_multiplier=-1).then_inc(const_set, 1)
            pool.wait_ge(const_set, 4)
            nc.gpsimd.tensor_copy(ident_r[:], ident[:]).then_inc(const_set, 1)

            def norm_lo(n, c):
                s, (at, cols) = norms[n], (FRAME_CHUNKS if n == 2 else ALL_CHUNKS)[c]
                for kt in range(KT):
                    if pool_splits(n, c, kt):
                        m = c * KT + kt
                        pool.wait_ge(s["hi"], m + 1)
                        nc.gpsimd.tensor_tensor(u_lo[:, kt, at:at + cols], un[:, m % 3, 0:cols],
                                                u_hi[:, kt, at:at + cols].bitcast(F32), ALU.subtract)\
                            .then_inc(s["lo_pool"], 1)

            def ffn(n):
                s = ffns[n]

                def split_gate_up(turn):
                    pool.wait_ge(s["g_hi"], turn + 1)
                    nc.gpsimd.tensor_tensor(wg[:, 1], stage_g, wg[:, 0].bitcast(F32), ALU.subtract)\
                        .then_inc(s["g_split"], 1)
                    pool.wait_ge(s["u_hi"], turn + 1)
                    nc.gpsimd.tensor_tensor(wu[:, 1], stage_u, wu[:, 0].bitcast(F32), ALU.subtract)\
                        .then_inc(s["u_split"], 1)

                def split_down(turn):
                    pool.wait_ge(s["d_hi"], turn + 1)
                    nc.gpsimd.tensor_tensor(wd[:, 1], stage_d, wd[:, 0].bitcast(F32), ALU.subtract)\
                        .then_inc(s["d_split"], 1)

                if n == 0:
                    norm_lo(0, 0)
                    split_gate_up(0)
                    norm_lo(0, 2)
                else:
                    split_gate_up(0)
                    norm_lo(2, 0)
                    norm_lo(2, 1)
                with pool.Fori(0, FF_PAIRS - 1) as i:
                    split_down(i)
                    split_gate_up(i + 1)
                split_down(FF_PAIRS - 1)

            ffn(0)

            def split_weights(unit, kind):
                dst = (wq, w_kv, w_kv, wo)[kind]
                src = stage_a[:, unit[0] % 2, :]
                if kind != 3:
                    src = src.rearrange("p (k f) -> p k f", k=KT)
                pool.wait_ge(a_hi, unit[0] + 1 + 4 * unit[1])
                nc.gpsimd.tensor_tensor(dst[:, 1], src, dst[:, 0].bitcast(F32), ALU.subtract)\
                    .then_inc(a_split, 1)

            def split_last(half):
                pool.wait_ge(a_hi, 4 * HEADS + half)
                nc.gpsimd.tensor_tensor(wo_last[half][:, 1], stage_a[:, 1, half * BANK:(half + 1) * BANK],
                                        wo_last[half][:, 0].bitcast(F32), ALU.subtract).then_inc(a_split, 1)

            def head(hd, last):
                for s in range(SLOTS):
                    if s < S:
                        n, rows = STEPS[s][3], META if STEPS[s][1] == META_TILE else P
                        pool.wait_ge(sp_hi_done, S * hd + s + 1)
                        nc.gpsimd.tensor_tensor(sp_lo[0:rows, s % 2, 0:n], sp[0:rows, s % 3, 0:n],
                                                sp_hi[0:rows, s % 2, 0:n].bitcast(F32), ALU.subtract)\
                            .then_inc(sp_lo_done, 1)
                    if 2 <= s < S + 2:
                        t = s - 2
                        n, rows = STEPS[t][3], META if STEPS[t][1] == META_TILE else P
                        pool.wait_ge(w_hi_done, S * hd + t + 1)
                        nc.gpsimd.tensor_tensor(w_lo[0:rows, t % 2, 0:n], wf[0:rows, t % 2, 0:n],
                                                w_hi[0:rows, t % 2, 0:n].bitcast(F32), ALU.subtract)\
                            .then_inc(w_lo_done, 1)
                    if s == 5 and not last:
                        split_weights((3, hd), 2)
                    if s == 9 and not last:
                        split_weights((4, hd), 0)
                    if last and s in LAST_O_SPLITS:
                        split_last(LAST_O_SPLITS.index(s))
                if not last:
                    split_weights((5, hd), 3)
                    split_weights((6, hd), 1)

            split_weights((0, 0), 2)
            split_weights((1, 0), 0)
            for c in range(len(ALL_CHUNKS)):
                norm_lo(1, c)
            split_weights((2, 0), 1)
            with pool.Fori(0, HEADS - 1) as hd:
                head(hd, last=False)
            head(HEADS - 1, last=True)

            ffn(1)

        @block.scalar
        def _(act):
            def take_high(c, kt):
                if kt:
                    return
                for t in X_TILES[c]:
                    cols = META if t == META_TILE else P
                    act.wait_ge(x_transposed, t + 1)
                    src = psum[:, 6 * (t % 2) + 1, :].rearrange("p (k c) -> p k c", k=4)[:, :, 0:cols]
                    nc.scalar.activation(h[:, 4:8, t * P:t * P + cols], src, ACT.Copy).then_inc(h_high, 1)
                act.wait_ge(h_high, X_TILES[c][-1] + 1)
                act.wait_ge(h_low, X_TILES[c][-1] + 1)

            def norm(n, chunks, tile_ready, meanwhile):
                s = norms[n]

                def square(c, kt):
                    m, (at, cols) = c * KT + kt, chunks[c]
                    wait(act, s["summed"], m - 2)
                    nc.scalar.activation(sq[:, m % 3, 0:cols], h[:, kt, at:at + cols], ACT.Square)\
                        .then_inc(s["squared"], 1)

                def root(c):
                    cols = chunks[c][1]
                    act.wait_ge(s["summed"], KT * (c + 1))
                    if c >= 2:
                        act.wait_ge(s["un"], KT * (c - 1))
                    nc.scalar.activation(rstd[:, c % 2, 0:cols], psum[:, NORM_BANKS[n] + c, 0:cols], ACT.Sqrt,
                                         scale=1.0 / D_MODEL, bias=eps[:, 0:1]).then_inc(s["root"], 1)

                def hi(c, kt):
                    m, (at, cols) = c * KT + kt, chunks[c]
                    act.wait_ge(s["un"], m + 1)
                    nc.scalar.activation(u_hi[:, kt, at:at + cols], un[:, m % 3, 0:cols], ACT.Copy)\
                        .then_inc(s["hi"], 1)

                nc.scalar.preload_act_table(ACT.Sqrt)
                if n == 2:
                    meanwhile("gate")
                ahead = len(chunks) - 1
                for c in range(ahead):
                    for kt in range(KT):
                        if n == 1 and c == 0 and kt == 3:
                            meanwhile()
                        tile_ready(c, kt)
                        square(c, kt)
                root(0)
                if n == 0:
                    tile_ready(ahead, 0)
                if n == 2:
                    meanwhile("up")
                if ahead > 1:
                    root(1)
                for kt in range(KT):
                    if n == 0 and kt == 5:
                        meanwhile("gate")
                    if n == 0:
                        square(ahead, kt)
                        hi(0, kt)
                    else:
                        hi(0, kt)
                        tile_ready(ahead, kt)
                        square(ahead, kt)
                if n == 0:
                    meanwhile("up")
                for c in range(1, len(chunks)):
                    if c > 1 or ahead == 1:
                        root(c)
                    for kt in range(KT):
                        hi(c, kt)
                norm_over(act, n)

            def split_gate(n, turn):
                s = ffns[n]
                act.wait_ge(s["g_loaded"], 16 * turn + 16)
                nc.scalar.activation(wg[:, 0], stage_g, ACT.Copy).then_inc(s["g_hi"], 1)

            def split_up(n, turn):
                s = ffns[n]
                act.wait_ge(s["u_loaded"], 16 * turn + 16)
                if n == 1 and isinstance(turn, int) and turn == 0:
                    act.wait_ge(evacuated, GROUPS_BEFORE_LAST_O)
                nc.scalar.activation(wu[:, 0], stage_u, ACT.Copy).then_inc(s["u_hi"], 1)

            def first_weights(n):
                return lambda which: split_gate(n, 0) if which == "gate" else split_up(n, 0)

            def ffn(n, chunks):
                s = ffns[n]
                per_turn = 2 * len(chunks)

                def turn(i, last):
                    for c, (at, cols) in enumerate(chunks):
                        for ft in range(2):
                            m = 2 * c + ft
                            act.wait_ge(s["gate"], per_turn * i + m + 1)
                            nc.scalar.activation(silu_g[:, m % 2, 0:cols], psum[:, 2 * (m % 2), 0:cols], ACT.Silu)\
                                .then_inc(s["silu"], 1)
                            act.wait_ge(s["hidden"], per_turn * i + m + 1)
                            nc.scalar.activation(hid_hi[:, ft, at:at + cols], hidden[:, m % 2, 0:cols], ACT.Copy)\
                                .then_inc(s["hid_hi"], 1)
                            if m == 0:
                                act.wait_ge(s["d_loaded"], 16 * i + 16)
                                nc.scalar.activation(wd[:, 0], stage_d, ACT.Copy).then_inc(s["d_hi"], 1)
                    if not last:
                        split_gate(n, i + 1)
                        split_up(n, i + 1)

                with act.Fori(0, FF_PAIRS - 1) as i:
                    turn(i, last=False)
                turn(FF_PAIRS - 1, last=True)

            act.wait_ge(eps_set, 1)
            norm(0, ALL_CHUNKS, take_high, first_weights(0))
            ffn(0, ALL_CHUNKS)

            def split_weights(unit, kind):
                dst = (wq, w_kv, w_kv, wo)[kind]
                src = stage_a[:, unit[0] % 2, :]
                if kind != 3:
                    src = src.rearrange("p (k f) -> p k f", k=KT)
                act.wait_ge(a_loaded[unit[0] % 2], 16 * (unit[0] // 2 + 1) + 32 * unit[1])
                nc.scalar.activation(dst[:, 0], src, ACT.Copy).then_inc(a_hi, 1)

            def split_last(half):
                act.wait_ge(a_loaded[1], 16 * 2 + 32 * (HEADS - 1))
                nc.scalar.activation(wo_last[half][:, 0], stage_a[:, 1, half * BANK:(half + 1) * BANK], ACT.Copy)\
                    .then_inc(a_hi, 1)

            def head(hd, first, last):
                base = group_base(hd)

                def group_ready(g):
                    act.wait_ge(grouped, base + g + 1)

                act.wait_ge(grouped, base)
                split_weights((2, 0) if first else (6, hd - 1), 1)
                group_ready(G_Q1)
                nc.scalar.activation(q[:, 0, BANK:], psum[:, Q1_BANK, :], ACT.Copy, scale=Q_SCALE)\
                    .then_inc(proj_hi, 1)
                for c, (t0, t1) in enumerate(VT_GROUPS):
                    rows = META if t0 == META_TILE else P
                    group_ready(G_VT + c)
                    src = psum[0:rows, VT_BANKS[c], 0:(t1 - t0) * P].rearrange("p (t d) -> p t d", d=P)
                    nc.scalar.activation(v[0:rows, 0, t0:t1, :], src, ACT.Copy).then_inc(proj_hi, 1)
                for n, c in enumerate(K_ORDER):
                    at, cols = ALL_CHUNKS[c]
                    group_ready(G_K + n)
                    nc.scalar.activation(k[:, 0, at:at + cols], psum[:, K_BANKS[n], 0:cols], ACT.Copy)\
                        .then_inc(proj_hi, 1)
                for s in range(SLOTS):
                    if s < S:
                        _, tile, _, n, _ = STEPS[s]
                        rows = META if tile == META_TILE else P
                        z, z_sb, e = psum[0:rows, s % 2, 0:n], zs[0:rows, s % 4, 0:n], sp[0:rows, s % 3, 0:n]
                        act.wait_ge(scored, S * hd + s + 1)
                        wait(act, w_done, S * hd + (s - 3 if s >= 4 else 0))
                        nc.scalar.activation(z_sb, z, ACT.Copy).then_inc(z_read, 1)
                        wait(act, sp_lo_done, S * hd + (s - 2 if s >= 3 else 0))
                        nc.scalar.activation(e, z, ACT.Abs).then_inc(z_read, 1)
                        act.wait_ge(z_read, 2 * (S * hd + s + 1))
                        nc.scalar.activation(e, e, ACT.Exp, scale=-1.0).then_inc(exped, 1)
                        act.wait_ge(exped, S * hd + s + 1)
                        nc.scalar.activation(e, e, ACT.Ln, bias=1.0).then_inc(logged, 1)
                    if 2 <= s < S + 2:
                        t = s - 2
                        n, rows = STEPS[t][3], META if STEPS[t][1] == META_TILE else P
                        act.wait_ge(logw_done, S * hd + t + 1)
                        wait(act, w_lo_done, S * hd + (t - 1 if t >= 2 else 0))
                        nc.scalar.activation(wf[0:rows, t % 2, 0:n], zs[0:rows, t % 4, 0:n], ACT.Exp)\
                            .then_inc(w_done, 1)
                    if s == KT - 1:
                        act.wait_ge(q0_grouped, hd + 1)
                        nc.scalar.activation(q[:, 0, 0:BANK], psum[:, Q0_BANK, :], ACT.Copy, scale=Q_SCALE)\
                            .then_inc(proj_hi, 1)
                    if s == 5 and not last:
                        split_weights((3, hd), 2)
                    if s == 9 and not last:
                        split_weights((4, hd), 0)
                    if last and s in LAST_O_SPLITS:
                        split_last(LAST_O_SPLITS.index(s))
                    for chunk, slot in ((1, LAST_OF_CHUNK[1] + 5), (0, SLOTS - 1)):
                        if s == slot:
                            act.wait_ge(weighed, S * hd + LAST_OF_CHUNK[chunk] + 1)
                            nc.scalar.activation(o[:, 0, chunk * BANK:(chunk + 1) * BANK], psum[:, 4 + chunk, :],
                                                 ACT.Copy).then_inc(o_hi_done, 1)
                if not first:
                    group_ready(G_O + O_GROUPS - 1)
                if not last:
                    split_weights((5, hd), 3)

            def split_first_weights():
                split_weights((0, 0), 2)
                split_weights((1, 0), 0)

            def h_ready(c, kt):
                act.wait_ge(ffns[0]["added"], KT * (len(ALL_CHUNKS) * (FF_PAIRS - 1) + c) + kt + 1)

            norm(1, ALL_CHUNKS, h_ready, split_first_weights)
            nc.scalar.preload_act_table_set("natural_log_exp_and_others")
            head(0, first=True, last=False)
            with act.Fori(1, HEADS - 1) as hd:
                head(hd, first=False, last=False)
            head(HEADS - 1, first=False, last=True)

            def h_ready_2(c, kt):
                act.wait_ge(evacuated, GROUPS_BEFORE_LAST_O + KT * c + kt + 1)

            norm(2, FRAME_CHUNKS, h_ready_2, first_weights(1))
            ffn(1, FRAME_CHUNKS)
            ffn_over(act, 1)

            for t in range(FRAMES // P):
                for half in range(2):
                    m = 2 * t + half
                    act.wait_ge(out_transposed, m + 1)
                    wait(act, out_squared, m - 1)
                    nc.scalar.activation(square_out[:, m % 2, :], psum[:, m % 8, :], ACT.Square,
                                         accum_out=stats[:, t, half:half + 1]).then_inc(out_squared, 1)
                act.wait_ge(out_total, t + 1)
                nc.scalar.activation(stats[:, t, 3:4], stats[:, t, 2:3], ACT.Sqrt, scale=1.0 / D_MODEL,
                                     bias=eps[:, 0:1]).then_inc(out_root, 1)

        @block.vector
        def _(dve):
            nc.vector.memset(eps[:], EPS).then_inc(eps_set, 1)
            for t in range(META_TILE + 1):
                cols = META if t == META_TILE else P
                dve.wait_ge(x_transposed, t + 1)
                src = psum[:, 6 * (t % 2), :].rearrange("p (k c) -> p k c", k=4)[:, :, 0:cols]
                nc.vector.tensor_copy(h[:, 0:4, t * P:t * P + cols], src).then_inc(h_low, 1)

            def norm(n, chunks, chunk_ready=None, between=None):
                s = norms[n]

                def lo(c, kt):
                    if pool_splits(n, c, kt):
                        return
                    m, (at, cols) = c * KT + kt, chunks[c]
                    dve.wait_ge(s["hi"], m + 1)
                    nc.vector.tensor_tensor(u_lo[:, kt, at:at + cols], un[:, m % 3, 0:cols],
                                            u_hi[:, kt, at:at + cols].bitcast(F32), ALU.subtract)\
                        .then_inc(s["lo"], 1)

                for c, (at, cols) in enumerate(chunks):
                    dve.wait_ge(s["root"], c + 1)
                    nc.vector.reciprocal(rstd[:, c % 2, 0:cols], rstd[:, c % 2, 0:cols]).then_inc(s["rstd"], 1)
                    dve.wait_ge(s["rstd"], c + 1)
                    if chunk_ready:
                        chunk_ready(c)
                    for kt in range(KT):
                        if between and c == 0:
                            between(kt)
                        m = c * KT + kt
                        split_through(dve, n, m - 3)
                        nc.vector.scalar_tensor_tensor(out=un[:, m % 3, 0:cols], in0=h[:, kt, at:at + cols],
                                                       scalar=gains[:, n, kt:kt + 1], in1=rstd[:, c % 2, 0:cols],
                                                       op0=ALU.mult, op1=ALU.mult).then_inc(s["un"], 1)
                        if kt:
                            lo(c, kt - 1)
                    lo(c, KT - 1)
                norm_over(dve, n)

            def add_share(n, chunks, i, c, dt):
                (at, cols), m = chunks[c], c * KT + dt
                dve.wait_ge(ffns[n]["down"], KT * len(chunks) * i + m + 1)
                nc.vector.scalar_tensor_tensor(out=h[:, dt, at:at + cols], in0=psum[:, 4 + m % 4, 0:cols],
                                               scalar=0.5, in1=h[:, dt, at:at + cols],
                                               op0=ALU.mult, op1=ALU.add).then_inc(ffns[n]["added"], 1)

            def ffn(n, chunks):
                s = ffns[n]
                per_turn = 2 * len(chunks)

                def turn(i, last):
                    for c, (at, cols) in enumerate(chunks):
                        for ft in range(2):
                            m = 2 * c + ft
                            dve.wait_ge(s["silu"], per_turn * i + m + 1)
                            dve.wait_ge(s["up"], per_turn * i + m + 1)
                            if m >= 2:
                                dve.wait_ge(s["hid_lo"], per_turn * i + m - 1)
                            nc.vector.tensor_tensor(hidden[:, m % 2, 0:cols], silu_g[:, m % 2, 0:cols],
                                                    psum[:, 2 * (m % 2) + 1, 0:cols], ALU.mult)\
                                .then_inc(s["hidden"], 1)
                            dve.wait_ge(s["hid_hi"], per_turn * i + m + 1)
                            nc.vector.tensor_tensor(hid_lo[:, ft, at:at + cols], hidden[:, m % 2, 0:cols],
                                                    hid_hi[:, ft, at:at + cols].bitcast(F32), ALU.subtract)\
                                .then_inc(s["hid_lo"], 1)
                    for c in range(len(chunks) - (1 if last and n == 0 else 0)):
                        for dt in range(KT):
                            add_share(n, chunks, i, c, dt)

                with dve.Fori(0, FF_PAIRS - 1) as i:
                    turn(i, last=False)
                turn(FF_PAIRS - 1, last=True)

            def take_v(c, groups_before, banks=V_BANKS):
                at, cols = ALL_CHUNKS[c]
                dve.wait_ge(grouped, groups_before + c + 1)
                nc.vector.tensor_copy(v_t[:, at:at + cols], psum[:, banks[c], 0:cols]).then_inc(evacuated, 1)

            def head(hd, first, last):
                base = group_base(hd)

                def group_ready(g):
                    dve.wait_ge(grouped, base + g + 1)

                def lo(dst, src, hi, scale=None, freed=evacuated):
                    if scale is None:
                        done = nc.vector.tensor_tensor(dst, src, hi.bitcast(F32), ALU.subtract)
                    else:
                        done = nc.vector.scalar_tensor_tensor(out=dst, in0=src, scalar=scale, in1=hi.bitcast(F32),
                                                              op0=ALU.mult, op1=ALU.subtract)
                    done.then_inc(freed, 1)

                dve.wait_ge(proj_hi, 8 * hd + 1)
                lo(q[:, 1, BANK:], psum[:, Q1_BANK, :], q[:, 0, BANK:], Q_SCALE)
                for c, (t0, t1) in enumerate(VT_GROUPS):
                    rows = META if t0 == META_TILE else P
                    dve.wait_ge(proj_hi, 8 * hd + 2 + c)
                    src = psum[0:rows, VT_BANKS[c], 0:(t1 - t0) * P].rearrange("p (t d) -> p t d", d=P)
                    lo(v[0:rows, 1, t0:t1, :], src, v[0:rows, 0, t0:t1, :])
                for n, c in enumerate(K_ORDER):
                    at, cols = ALL_CHUNKS[c]
                    dve.wait_ge(proj_hi, 8 * hd + 5 + n)
                    lo(k[:, 1, at:at + cols], psum[:, K_BANKS[n], 0:cols], k[:, 0, at:at + cols])
                for s in range(SLOTS):
                    if 2 <= s < S + 2:
                        t = s - 2
                        chunk, tile, at, n, _ = STEPS[t]
                        rows = META if tile == META_TILE else P
                        at -= chunk * BANK
                        dve.wait_ge(summed, S * hd + t + 1)
                        nc.vector.tensor_tensor(zs[0:rows, t % 4, 0:n], zs[0:rows, t % 4, 0:n],
                                                psum[0:rows, 2 + chunk, at:at + n], ALU.subtract)\
                            .then_inc(logw_done, 1)
                    if s < S:
                        n, rows = STEPS[s][3], META if STEPS[s][1] == META_TILE else P
                        e = sp[0:rows, s % 3, 0:n]
                        dve.wait_ge(logged, S * hd + s + 1)
                        nc.vector.scalar_tensor_tensor(out=e, in0=zs[0:rows, s % 4, 0:n], scalar=0.0, in1=e,
                                                       op0=ALU.max, op1=ALU.add).then_inc(softplused, 1)
                    if s < O_GROUPS and not first:
                        group_ready(G_O + s)
                        add_output(s, O_BANK)
                    if s < S:
                        dve.wait_ge(softplused, S * hd + s + 1)
                        if s >= 2 and STEPS[s - 2][1] == META_TILE:
                            dve.wait_ge(summed, S * hd + s - 1)
                        elif s >= 2:
                            dve.wait_ge(completed, COMPLETIONS * hd + completions_before(s - 1))
                        nc.vector.tensor_copy(sp_hi[0:rows, s % 2, 0:n], e).then_inc(sp_hi_done, 1)
                    if 2 <= s < S + 2:
                        t = s - 2
                        n, rows = STEPS[t][3], META if STEPS[t][1] == META_TILE else P
                        dve.wait_ge(w_done, S * hd + t + 1)
                        wait(dve, weighed, S * hd + (t - 1 if t >= 2 else 0))
                        nc.vector.tensor_copy(w_hi[0:rows, t % 2, 0:n], wf[0:rows, t % 2, 0:n])\
                            .then_inc(w_hi_done, 1)
                    if s == KT - 1:
                        dve.wait_ge(proj_hi, 8 * hd + 8)
                        lo(q[:, 1, 0:BANK], psum[:, Q0_BANK, :], q[:, 0, 0:BANK], Q_SCALE, q0_evacuated)
                    if s == SLOTS - 1 and not last:
                        take_v(0, base + first_v_group(first))
                        take_v(1, base + first_v_group(first))
                    for chunk, slot in ((1, LAST_OF_CHUNK[1] + 5), (0, SLOTS - 1)):
                        if s == slot:
                            cols = slice(chunk * BANK, (chunk + 1) * BANK)
                            dve.wait_ge(o_hi_done, 2 * hd + 2 - chunk)
                            nc.vector.tensor_tensor(o[:, 1, cols], psum[:, 4 + chunk, :], o[:, 0, cols].bitcast(F32),
                                                    ALU.subtract).then_inc(o_lo_done, 1)
                if not last:
                    take_v(2, base + first_v_group(first))

            def add_output(g, bank):
                dt, chunk = g % KT, 1 - g // KT
                cols = slice(chunk * BANK, (chunk + 1) * BANK)
                nc.vector.tensor_tensor(h[:, dt, cols], psum[:, bank, :], h[:, dt, cols], ALU.add)\
                    .then_inc(evacuated, 1)

            dve.wait_ge(gains_loaded, 16)
            dve.wait_ge(h_low, META_TILE + 1)
            dve.wait_ge(h_high, META_TILE + 1)
            norm(0, ALL_CHUNKS)
            ffn(0, ALL_CHUNKS)

            def ffn_added(c):
                dve.wait_ge(ffns[0]["added"], KT * (len(ALL_CHUNKS) * (FF_PAIRS - 1) + c + 1))

            norm(1, ALL_CHUNKS, ffn_added,
                 lambda kt: add_share(0, ALL_CHUNKS, FF_PAIRS - 1, len(ALL_CHUNKS) - 1, kt))
            for c in range(V_GROUPS):
                take_v(c, 0, FIRST_V_BANKS)
            head(0, first=True, last=False)
            with dve.Fori(1, HEADS - 1) as hd:
                head(hd, first=False, last=False)
            head(HEADS - 1, first=False, last=True)

            def add_last_output(n):
                g = LAST_O_ORDER[n]
                dve.wait_ge(grouped, GROUPS_BEFORE_LAST_O + n + 1)
                add_output(g, LAST_O_BANKS[n % len(LAST_O_BANKS)])

            def output_added(c):
                dve.wait_ge(evacuated, GROUPS_BEFORE_LAST_O + KT * (c + 1))

            def add_rest(kt):
                if KT + LAST_O_AHEAD + kt < O_GROUPS:
                    add_last_output(KT + LAST_O_AHEAD + kt)

            for n in range(KT + LAST_O_AHEAD):
                add_last_output(n)
            norm(2, FRAME_CHUNKS, output_added, add_rest)
            ffn(1, FRAME_CHUNKS)

            dve.wait_ge(gain_loaded, 16)

            def scale_rows(t):
                if t >= 4:
                    dve.wait_ge(out_stored[t % 4], 16 * (t // 4))
                dve.wait_ge(out_rstd, t + 1)
                for half in range(2):
                    cols = slice(half * BANK, (half + 1) * BANK)
                    nc.vector.scalar_tensor_tensor(out=out_tiles[:, t % 4, cols], in0=psum[:, (2 * t + half) % 8, :],
                                                   scalar=stats[:, t, 3:4], in1=gain_row[:, cols],
                                                   op0=ALU.mult, op1=ALU.mult).then_inc(out_scaled, 1)

            for t in range(FRAMES // P):
                dve.wait_ge(out_squared, 2 * t + 2)
                nc.vector.tensor_tensor(stats[:, t, 2:3], stats[:, t, 0:1], stats[:, t, 1:2], ALU.add)\
                    .then_inc(out_total, 1)
                if t:
                    scale_rows(t - 1)
                dve.wait_ge(out_root, t + 1)
                nc.vector.reciprocal(stats[:, t, 3:4], stats[:, t, 3:4]).then_inc(out_rstd, 1)
            scale_rows(FRAMES // P - 1)

        @block.tensor
        def _(pe):
            def product(dst, w_halves, x_halves, start, stop):
                (wh, wl), (xh, xl) = w_halves, x_halves
                nc.tensor.matmul(dst, wh, xh, start=start, stop=False, skip_group_check=True)
                nc.tensor.matmul(dst, wh, xl, start=False, stop=False, skip_group_check=True)
                return nc.tensor.matmul(dst, wl, xh, start=False, stop=stop, skip_group_check=True)

            def transpose_x(c):
                for t in X_TILES[c]:
                    rows = META if t == META_TILE else P
                    pe.wait_ge(x_loaded[t % 4], 16 * (t // 4 + 1))
                    if t >= 2:
                        pe.wait_ge(h_low, t - 1)
                        pe.wait_ge(h_high, t - 1)
                    for kt in range(KT):
                        dst = psum[:, 6 * (t % 2) + kt // 4, (kt % 4) * P:(kt % 4) * P + rows]
                        last = nc.tensor.transpose(dst, x_tiles[0:rows, t % 4, kt * P:(kt + 1) * P],
                                                   ident[0:rows, 0:rows])
                    last.then_inc(x_transposed, 1)

            def sums(n, c, kts=range(KT)):
                s = norms[n]
                cols = (FRAME_CHUNKS if n == 2 else ALL_CHUNKS)[c][1]
                for kt in kts:
                    m = c * KT + kt
                    pe.wait_ge(s["squared"], m + 1)
                    nc.tensor.matmul(psum[:, NORM_BANKS[n] + c, 0:cols], ones[:], sq[:, m % 3, 0:cols],
                                     start=kt == 0, stop=kt == KT - 1).then_inc(s["summed"], 1)

            def ffn(n, chunks):
                s = ffns[n]
                per_turn, adds = 2 * len(chunks), KT * len(chunks)

                def gate_up(i):
                    for c, (at, cols) in enumerate(chunks):
                        for ft in range(2):
                            m = 2 * c + ft
                            if m >= 2:
                                pe.wait_ge(s["hidden"], per_turn * i + m - 1)
                            for w, split, done, bank in ((wg, "g_split", "gate", 0), (wu, "u_split", "up", 1)):
                                if m == 0:
                                    pe.wait_ge(s[split], i + 1)
                                f = slice(ft * P, (ft + 1) * P)
                                for kt in range(KT):
                                    if ft == bank == 0 and kt % 4 == 0:
                                        split_through(pe, n * 2, KT * c + kt + 3)
                                    last = product(psum[:, 2 * (m % 2) + bank, 0:cols],
                                                   (w[:, 0, kt, f], w[:, 1, kt, f]),
                                                   (u_hi[:, kt, at:at + cols], u_lo[:, kt, at:at + cols]),
                                                   start=kt == 0, stop=kt == KT - 1)
                                last.then_inc(s[done], 1)
                    pe.wait_ge(s["d_split"], i + 1)

                def down(i, c):
                    at, cols = chunks[c]
                    pe.wait_ge(s["hid_lo"], per_turn * i + 2 * c + 2)
                    for dt in range(KT):
                        m = c * KT + dt
                        if m >= 4:
                            pe.wait_ge(s["added"], adds * i + m - 3)
                        d = slice(dt * P, (dt + 1) * P)
                        for ft in range(2):
                            last = product(psum[:, 4 + m % 4, 0:cols], (wd[:, 0, ft, d], wd[:, 1, ft, d]),
                                           (hid_hi[:, ft, at:at + cols], hid_lo[:, ft, at:at + cols]),
                                           start=ft == 0, stop=ft == 1)
                        last.then_inc(s["down"], 1)

                with pe.Fori(0, FF_PAIRS - 1) as i:
                    gate_up(i)
                    for c in range(len(chunks)):
                        down(i, c)
                gate_up(FF_PAIRS - 1)
                down(FF_PAIRS - 1, 0)
                down(FF_PAIRS - 1, 1)
                if n == 0:
                    sums(1, 0)
                    sums(1, 1)
                    down(FF_PAIRS - 1, 2)

            def output_group(g, bank, last=False):
                dt, chunk = g % KT, 1 - g // KT
                cols, d = slice(chunk * BANK, (chunk + 1) * BANK), slice(dt * P, (dt + 1) * P)
                w = wo[:, :, d]
                if last:
                    w = wo_last[dt // 4][:, :, dt % 4 * P:(dt % 4 + 1) * P]
                product(psum[:, bank, :], (w[:, 0], w[:, 1]),
                        (o[:, 0, cols], o[:, 1, cols]), start=True, stop=True).then_inc(grouped, 1)

            def project(bank, w, at, cols, kts, done):
                for kt in kts:
                    last = product(psum[:, bank, 0:cols], (w[:, 0, kt, :], w[:, 1, kt, :]),
                                   (u_hi[:, kt, at:at + cols], u_lo[:, kt, at:at + cols]),
                                   start=kt == 0, stop=kt == KT - 1)
                if kts[-1] == KT - 1:
                    last.then_inc(done, 1)

            def project_v(c):
                project(V_BANKS[c], w_kv, *ALL_CHUNKS[c], range(KT), grouped)

            def head(hd, first, last):
                base = group_base(hd)

                def bank_free(g):
                    pe.wait_ge(evacuated, base + g - 1)

                units = 4 * hd
                bank_free(G_Q1)
                pe.wait_ge(a_split, 2 if first else units + 1)
                project(Q1_BANK, wq, BANK, BANK, range(KT), grouped)
                pe.wait_ge(evacuated, base)
                for c, (t0, t1) in enumerate(VT_GROUPS):
                    for t in range(t0, t1):
                        rows = META if t == META_TILE else P
                        dst = psum[0:rows, VT_BANKS[c], (t - t0) * P:(t - t0 + 1) * P]
                        done = nc.tensor.transpose(dst, v_t[:, t * P:t * P + rows], ident[:])
                    done.then_inc(grouped, 1)
                pe.wait_ge(a_split, units + 3)
                for n, c in enumerate(K_ORDER):
                    if n == 1:
                        pe.wait_ge(evacuated, base + 1)
                    project(K_BANKS[n], w_kv, *ALL_CHUNKS[c], range(KT), grouped)

                def score(t):
                    _, tile, at, n, mask_at = STEPS[t]
                    rows = META if tile == META_TILE else P
                    keys = slice(tile * P, tile * P + rows)
                    if t < 2:
                        pe.wait_ge(evacuated, base + G_O - 1 + t)
                    if t == LAST_OF_CHUNK[1] + 1:
                        pe.wait_ge(q0_evacuated, hd + 1)
                    if t >= 2:
                        pe.wait_ge(z_read, 2 * (S * hd + t - 1))
                    dst = psum[0:rows, t % 2, 0:n]
                    last = product(dst, (k[:, 0, keys], k[:, 1, keys]), (q[:, 0, at:at + n], q[:, 1, at:at + n]),
                                   start=True, stop=mask_at is None)
                    if mask_at is not None:
                        last = nc.tensor.matmul(psum[:, t % 2, 0:2 * P], ident_r[:], mask[:, mask_at:mask_at + 2 * P],
                                                start=False, stop=True, skip_group_check=True)
                    last.then_inc(scored, 1)

                def running_sum(t, triangle, start, stop):
                    chunk, tile, at, n, _ = STEPS[t]
                    rows = META if tile == META_TILE else P
                    at -= chunk * BANK
                    dst = psum[:, 2 + chunk, at:at + n]
                    nc.tensor.matmul(dst, triangle[0:rows, :], sp_hi[0:rows, t % 2, 0:n],
                                     start=start, stop=False, skip_group_check=True)
                    return nc.tensor.matmul(dst, triangle[0:rows, :], sp_lo[0:rows, t % 2, 0:n],
                                            start=False, stop=stop, skip_group_check=True)

                def weigh(t):
                    chunk, tile, at, n, _ = STEPS[t]
                    rows = META if tile == META_TILE else P
                    at -= chunk * BANK
                    start = t == 0 or STEPS[t - 1][0] != chunk
                    if t == 0:
                        pe.wait_ge(evacuated, base + G_O)
                    if start:
                        wait(pe, o_lo_done, 2 * hd - chunk)
                    pe.wait_ge(w_lo_done, S * hd + t + 1)
                    product(psum[:, 4 + chunk, at:at + n], (v[0:rows, 0, tile, :], v[0:rows, 1, tile, :]),
                            (w_hi[0:rows, t % 2, 0:n], w_lo[0:rows, t % 2, 0:n]),
                            start=start, stop=tile == META_TILE).then_inc(weighed, 1)

                for s in range(SLOTS):
                    if s < S:
                        score(s)
                    if s < KT:
                        project(Q0_BANK, wq, 0, BANK, range(s, s + 1), q0_grouped)
                    t = s - 2
                    if 0 <= t < S:
                        start = t == 0 or STEPS[t - 1][0] != STEPS[t][0]
                        pe.wait_ge(sp_lo_done, S * hd + t + 1)
                        running_sum(t, tri, start, STEPS[t][1] == META_TILE).then_inc(summed, 1)
                    if V_FIRST_SLOT <= s < V_SLOT and not last:
                        kt = s - V_FIRST_SLOT
                        if kt == 0:
                            pe.wait_ge(a_split, units + 4)
                            pe.wait_ge(q0_evacuated, hd + 1)
                        project(V_BANKS[0], w_kv, *ALL_CHUNKS[0], range(kt, kt + 1), grouped)
                    if 0 <= s - 4 < S:
                        weigh(s - 4)
                    if s < O_GROUPS and not first:
                        if s == 0:
                            pe.wait_ge(a_split, units + 2)
                            pe.wait_ge(o_lo_done, 2 * hd)
                        if s:
                            pe.wait_ge(evacuated, base + G_O + s)
                        output_group(s, O_BANK)
                    if 0 <= t < S and STEPS[t][1] != META_TILE:
                        pe.wait_ge(logw_done, S * hd + t + 1)
                        running_sum(t, tri_rest, False, False).then_inc(completed, 1)
                    if V_SLOT <= s + 1 < V_SLOT + V_GROUPS - 1 and not last:
                        c = s + 2 - V_SLOT
                        bank_free(first_v_group(first) + c)
                        project_v(c)

            pe.wait_ge(const_set, CONSTANTS)
            for c in range(len(ALL_CHUNKS)):
                transpose_x(c)
                sums(0, c)
            ffn(0, ALL_CHUNKS)
            sums(1, 2)
            pe.wait_ge(a_split, 1)
            for c in range(V_GROUPS):
                for kt in range(KT):
                    split_through(pe, 1, KT * c + kt)
                    project(FIRST_V_BANKS[c], w_kv, *ALL_CHUNKS[c], range(kt, kt + 1), grouped)
            head(0, first=True, last=False)
            with pe.Fori(1, HEADS - 1) as hd:
                head(hd, first=False, last=False)
            head(HEADS - 1, first=False, last=True)
            pe.wait_ge(a_split, 4 * HEADS)
            pe.wait_ge(o_lo_done, 2 * HEADS)
            for n, g in enumerate(LAST_O_ORDER):
                if n == 4:
                    pe.wait_ge(a_split, 4 * HEADS + 1)
                pe.wait_ge(evacuated, GROUPS_BEFORE_LAST_O + max(0, n + 1 - len(LAST_O_BANKS)))
                output_group(g, LAST_O_BANKS[n % len(LAST_O_BANKS)], last=True)
                if LAST_O_AHEAD <= n + 1 < LAST_O_AHEAD + KT:
                    sums(2, 0, [n + 1 - LAST_O_AHEAD])
            sums(2, 1)
            ffn(1, FRAME_CHUNKS)

            ffn_over(pe, 1)
            for t in range(FRAMES // P):
                if t >= 4:
                    pe.wait_ge(out_scaled, 2 * (t - 3))
                for kt in range(KT):
                    last = nc.tensor.transpose(psum[:, (2 * t + kt // 4) % 8, (kt % 4) * P:(kt % 4 + 1) * P],
                                               h[:, kt, t * P:(t + 1) * P], ident[:])
                    if kt % 4 == 3:
                        last.then_inc(out_transposed, 1)


def kernel(**inputs):
    import numpy as np
    import concourse.bacc as bacc
    from concourse.bass_utils import run_bass_kernel_spmd

    nc = bacc.Bacc("TRN2", target_bir_lowering=False, num_devices=1)
    gains = np.stack([np.asarray(inputs[name][0]).reshape(KT, P).T for name in ("ffn1_norm", "mix_norm", "ffn2_norm")],
                     axis=1)
    arrays = {
        "x": inputs["x"][0], "meta": inputs["meta_tokens"],
        "gains": gains, "w1_in": inputs["ffn1_w_in"][0], "w1_out": inputs["ffn1_w_out"][0],
        "w2_in": inputs["ffn2_w_in"][0], "w2_out": inputs["ffn2_w_out"][0],
        "w_qkv": inputs["sb_w_qkv"][0], "w_o": inputs["sb_w_o"][0], "g_final": inputs["final_norm"],
    }
    arrays = {name + "_dram": np.ascontiguousarray(a) for name, a in arrays.items()}
    args = [nc.dram_tensor(name, a.shape, mybir.dt.from_np(a.dtype), kind="ExternalInput").ap()
            for name, a in arrays.items()]
    out = nc.dram_tensor("out_dram", (FRAMES, D_MODEL), F32, kind="ExternalOutput").ap()
    build(nc, *args, out)
    r = run_bass_kernel_spmd(nc, [arrays], core_ids=[0])
    return r.results[0]["out_dram"].reshape(1, FRAMES, D_MODEL)
```
